# Optimizing a Trainium2 kernel written in Bass

```python
import jax, jax.numpy as jnp
from jax import lax
import numpy as np

D_MODEL = 1024
BATCH = 1
SEQ = 1024
DEPTH = 1

MIX_WIDTH = D_MODEL
CONV_WIDTH = MIX_WIDTH // 2
CONV_GROUPS = 8
CONV_GROUP_DIM = CONV_WIDTH // CONV_GROUPS
CONV_K = 3
SB_WIDTH = MIX_WIDTH - CONV_WIDTH
SB_HEADS = 8
SB_HEAD_DIM = SB_WIDTH // SB_HEADS
Q_BLOCK = 128
PROJ_WIDTH = 3 * CONV_WIDTH + 3 * SB_WIDTH
N_GROUPS = 4
EXPERTS_PER_GROUP = 8
N_EXPERTS = N_GROUPS * EXPERTS_PER_GROUP
TOP_K = 2
D_EXPERT = D_MODEL // 2
DISPATCH_BLOCK = 256
EPS = 1e-6

kernel_name = "hymba_conv_stickbreak_hiermoe"

def rms_norm(x, g):
    xf = x.astype(jnp.float32)
    y = xf * lax.rsqrt(jnp.mean(xf * xf, axis=-1, keepdims=True) + EPS)
    return (y * g.astype(jnp.float32)).astype(x.dtype)

def short_conv_mixer(gate_b, gate_c, h, conv_w):
    u = gate_c * h
    T = u.shape[1]
    up = jnp.pad(u, ((0, 0), (CONV_K - 1, 0), (0, 0)))
    y = sum(conv_w[i] * up[:, i:i + T] for i in range(CONV_K))
    return gate_b * y

def stick_breaking_attention(q, k, v):
    S = q.shape[2]
    scale = 1.0 / float(np.sqrt(SB_HEAD_DIM))
    outs = []
    for blk in range(S // Q_BLOCK):
        t0 = blk * Q_BLOCK
        L = t0 + Q_BLOCK
        qb = q[:, :, t0:L].astype(jnp.float32)
        kb = k[:, :, :L].astype(jnp.float32)
        vb = v[:, :, :L].astype(jnp.float32)
        z = jnp.einsum('bhqd,bhkd->bhqk', qb, kb) * scale
        t_idx = t0 + jnp.arange(Q_BLOCK)[:, None]
        s_idx = jnp.arange(L)[None, :]
        mask = s_idx < t_idx
        log_keep = jnp.where(mask, jax.nn.log_sigmoid(-z), 0.0)
        shifted = jnp.concatenate([log_keep[..., 1:], jnp.zeros_like(log_keep[..., :1])], axis=-1)
        suffix = lax.cumsum(shifted, axis=3, reverse=True)
        A = jnp.where(mask, jnp.exp(jax.nn.log_sigmoid(z) + suffix), 0.0)
        outs.append(jnp.einsum('bhqk,bhkd->bhqd', A, vb).astype(v.dtype))
    return jnp.concatenate(outs, axis=2)

def hierarchical_moe(xn, w_group, b_group, w_expert, b_expert, w1, w3, w2):
    Bsz, T, D = xn.shape
    N = Bsz * T
    xf = xn.reshape(N, D)
    g_logits = (xf @ w_group).astype(jnp.float32) + b_group.astype(jnp.float32)
    g_prob = jax.nn.softmax(g_logits, axis=-1)
    g_idx = jnp.argmax(g_logits, axis=-1).astype(jnp.int32)
    p_g = jnp.take_along_axis(g_prob, g_idx[:, None], axis=-1)
    e_logits = ((xf @ w_expert).astype(jnp.float32) + b_expert.astype(jnp.float32)).reshape(N, N_GROUPS, EXPERTS_PER_GROUP)
    e_in_group = jnp.take_along_axis(e_logits, g_idx[:, None, None], axis=1)[:, 0]
    top_v, top_i = lax.top_k(e_in_group, TOP_K)
    gate = (p_g * jax.nn.softmax(top_v, axis=-1)).reshape(-1)
    eid = (g_idx[:, None] * EXPERTS_PER_GROUP + top_i).reshape(-1).astype(jnp.int32)
    tok = jnp.repeat(jnp.arange(N, dtype=jnp.int32), TOP_K)
    NK = N * TOP_K
    e_s, tok_s, gate_s = lax.sort((eid, tok, gate), num_keys=1)
    counts = jnp.bincount(eid, length=N_EXPERTS).astype(jnp.int32)
    start = jnp.cumsum(counts) - counts
    pcounts = (counts + DISPATCH_BLOCK - 1) // DISPATCH_BLOCK * DISPATCH_BLOCK
    pend = jnp.cumsum(pcounts)
    pstart = pend - pcounts
    dest = pstart[e_s] + jnp.arange(NK, dtype=jnp.int32) - start[e_s]
    n_blocks = -(-NK // DISPATCH_BLOCK) + N_EXPERTS
    P = n_blocks * DISPATCH_BLOCK
    buf_tok = jnp.full((P,), N, dtype=jnp.int32).at[dest].set(tok_s)
    buf_gate = jnp.zeros((P,), jnp.float32).at[dest].set(gate_s)
    blk_start = jnp.arange(n_blocks, dtype=jnp.int32) * DISPATCH_BLOCK
    blk_e = jnp.clip(jnp.searchsorted(pend, blk_start, side='right'), 0, N_EXPERTS - 1).astype(jnp.int32)
    x_pad = jnp.concatenate([xf, jnp.zeros((1, D), xf.dtype)], axis=0)
    xin = x_pad[buf_tok].reshape(n_blocks, DISPATCH_BLOCK, D)

    def expert_block(args):
        xb, e = args
        h = jax.nn.silu(xb @ w1[e]) * (xb @ w3[e])
        return h @ w2[e]

    y = lax.map(expert_block, (xin, blk_e)).reshape(P, D).astype(jnp.float32)
    out = jnp.zeros((N + 1, D), jnp.float32).at[buf_tok].add(y * buf_gate[:, None])[:N]
    return out.astype(xn.dtype).reshape(Bsz, T, D)

def setup_inputs(seed: int = 0) -> dict:
    key = jax.random.key(seed)
    ks = jax.random.split(key, 20)
    f32 = jnp.float32
    nrm = lambda k, shape, s: jax.random.normal(k, shape, f32) * s
    gain = lambda k, shape: 1.0 + 0.02 * jax.random.normal(k, shape, f32)
    return {
        "x": jax.random.normal(ks[0], (BATCH, SEQ, D_MODEL), f32),
        "norm_mix_w": gain(ks[1], (DEPTH, D_MODEL)),
        "w_in": nrm(ks[2], (DEPTH, D_MODEL, PROJ_WIDTH), D_MODEL ** -0.5),
        "conv_w": nrm(ks[3], (DEPTH, CONV_K, CONV_WIDTH), CONV_K ** -0.5),
        "q_norm_w": gain(ks[4], (DEPTH, SB_HEAD_DIM)),
        "k_norm_w": gain(ks[5], (DEPTH, SB_HEAD_DIM)),
        "group_norm_conv_w": gain(ks[6], (DEPTH, CONV_GROUPS, CONV_GROUP_DIM)),
        "group_norm_attn_w": gain(ks[7], (DEPTH, SB_HEADS, SB_HEAD_DIM)),
        "w_out": nrm(ks[8], (DEPTH, MIX_WIDTH, D_MODEL), MIX_WIDTH ** -0.5),
        "norm_ffn_w": gain(ks[9], (DEPTH, D_MODEL)),
        "w_group": nrm(ks[10], (DEPTH, D_MODEL, N_GROUPS), D_MODEL ** -0.5),
        "b_group": nrm(ks[11], (DEPTH, N_GROUPS), 0.01),
        "w_expert": nrm(ks[12], (DEPTH, D_MODEL, N_EXPERTS), D_MODEL ** -0.5),
        "b_expert": nrm(ks[13], (DEPTH, N_EXPERTS), 0.01),
        "w1": nrm(ks[14], (DEPTH, N_EXPERTS, D_MODEL, D_EXPERT), D_MODEL ** -0.5),
        "w3": nrm(ks[15], (DEPTH, N_EXPERTS, D_MODEL, D_EXPERT), D_MODEL ** -0.5),
        "w2": nrm(ks[16], (DEPTH, N_EXPERTS, D_EXPERT, D_MODEL), D_EXPERT ** -0.5),
    }

def reference(x, norm_mix_w, w_in, conv_w, q_norm_w, k_norm_w, group_norm_conv_w, group_norm_attn_w, w_out, norm_ffn_w, w_group, b_group, w_expert, b_expert, w1, w3, w2):
    Bsz, S, _ = x.shape
    for l in range(DEPTH):
        xn = rms_norm(x, norm_mix_w[l])
        proj = xn @ w_in[l]
        c_b, c_c, c_h = jnp.split(proj[..., :3 * CONV_WIDTH], 3, axis=-1)
        q, k, v = jnp.split(proj[..., 3 * CONV_WIDTH:], 3, axis=-1)
        yc = short_conv_mixer(c_b, c_c, c_h, conv_w[l])
        yc = rms_norm(yc.reshape(Bsz, S, CONV_GROUPS, CONV_GROUP_DIM), group_norm_conv_w[l]).reshape(Bsz, S, CONV_WIDTH)
        to_heads = lambda t: t.reshape(Bsz, S, SB_HEADS, SB_HEAD_DIM)
        qh = rms_norm(to_heads(q), q_norm_w[l]).transpose(0, 2, 1, 3)
        kh = rms_norm(to_heads(k), k_norm_w[l]).transpose(0, 2, 1, 3)
        vh = to_heads(v).transpose(0, 2, 1, 3)
        ya = stick_breaking_attention(qh, kh, vh).transpose(0, 2, 1, 3)
        ya = rms_norm(ya, group_norm_attn_w[l]).reshape(Bsz, S, SB_WIDTH)
        x = x + jnp.concatenate([yc, ya], axis=-1) @ w_out[l]
        x = x + hierarchical_moe(rms_norm(x, norm_ffn_w[l]), w_group[l], b_group[l], w_expert[l], b_expert[l], w1[l], w3[l], w2[l])
    return x


_drawn_inputs = setup_inputs


def setup_inputs(seed=0):
    import zlib

    import numpy as np

    out = dict(_drawn_inputs(seed))
    spreads = {}
    factors = {'q_norm_w': 4.857,
     'k_norm_w': 4.541,
     'group_norm_conv_w': 3.256,
     'group_norm_attn_w': 3.355,
     'norm_ffn_w': 3.024,
     'b_group': 6.345,
     'b_expert': 5.432}
    for name, (base, spread) in spreads.items():
        noise = np.random.default_rng([zlib.crc32(name.encode()), seed]).standard_normal(out[name].shape)
        drawn = base * np.exp(spread * noise) if base else spread * noise
        out[name] = __import__('jax').numpy.asarray(drawn.astype(out[name].dtype))
    for name, factor in factors.items():
        out[name] = (out[name] * factor).astype(out[name].dtype)
    return out
```

```python
from contextlib import ExitStack

import concourse.bass as bass
from concourse import mybir

F32 = mybir.dt.float32
F32R = mybir.dt.float32r
BF16 = mybir.dt.bfloat16
I32 = mybir.dt.int32
U32 = mybir.dt.uint32
ALU = mybir.AluOpType
ACT = mybir.ActivationFunctionType
AX = mybir.AxisListType

P = 128
BANK = 512
EPS = 1e-6
MASKED = -1e30
KIB = 1024


def hymba_moe_layer(nc, x, norm_mix_w, w_in, conv_w, q_norm_w, k_norm_w, group_norm_conv_w,
                    group_norm_attn_w, w_out, norm_ffn_w, w_group, b_group, w_expert, b_expert,
                    w1, w3, w2, out):
    S, D = x.shape[1], x.shape[2]
    KT = D // P
    NT = S // P
    CW = conv_w.shape[2]
    CB = CW // P
    TAPS = conv_w.shape[1]
    HD = q_norm_w.shape[1]
    NCH = w_in.shape[2] // CW
    HALVES = S // BANK
    NG = w_group.shape[2]
    NE = w_expert.shape[2]
    EPG = NE // NG
    F = w1.shape[3]
    FT = F // P
    PAIRS = 2 * S
    NBLK = S // P
    OVER = PAIRS // P - 1
    LOG = NG + NE
    assert D == S == KT * P and CW == 4 * P and NCH == 6 and HALVES == 2 and F == BANK

    xv = x.rearrange("a (m p) d -> (a m) p d", p=P)
    outv = out.rearrange("a (m p) d -> (a m) p d", p=P)
    w_in_v = w_in.rearrange("a (p k) n -> p (a k) n", k=KT)
    w_out_v = w_out.rearrange("a (c p) n -> p (a c) n", p=P)
    w1_v = w1.rearrange("a e (p k) f -> (a e) p k f", k=KT)
    w3_v = w3.rearrange("a e (p k) f -> (a e) p k f", k=KT)
    w2_v = w2.rearrange("a e (p k) n -> (a e) p k n", k=FT)

    xn2_rows = nc.dram_tensor("xn2_rows", (S, D), F32, kind="Internal").ap()
    y_rows = nc.dram_tensor("y_rows", (PAIRS, D), F32, kind="Internal").ap()

    with ExitStack() as ctx:
        sem = lambda name: ctx.enter_context(nc.semaphore(name))
        ps_t = ctx.enter_context(nc.psum_tensor("ps", [P, 8, BANK], F32))
        ps = ps_t[:]

        base = (nc.sbuf_base + 31) // 32 * 32
        ROOM = 205 * KIB
        ctx.enter_context(nc.sbuf_tensor("arena", [P, ROOM // 4], F32))
        names = set()

        def at(name, kib, shape, dt=F32):
            size = 4
            for n in shape[1:]:
                size *= n
            if dt == BF16:
                size //= 2
            assert name not in names and kib * KIB + size <= ROOM, name
            names.add(name)
            return nc.alloc_sbuf_tensor_at(name, shape, dt, offset=int(base + kib * KIB))[:]

        xnT_hi = at("xnT_hi", 0, [P, KT, S], F32R)
        xnT_lo = at("xnT_lo", 32, [P, KT, S], F32R)
        w_raw = [at(f"w_raw{i}", 64 + 8 * i, [P, 4, CW]) for i in range(2)]
        w_hi = at("w_hi", 80, [P, 4, CW], F32R)
        w_lo = at("w_lo", 88, [P, 4, CW], F32R)
        W1 = [at(f"W1_{i}", 48 * i, [P, KT, F]) for i in range(2)]
        W3 = [at(f"W3_{i}", 48 * i + 16, [P, KT, F]) for i in range(2)]
        W2 = [at(f"W2_{i}", 48 * i + 32, [P, FT, D]) for i in range(2)]
        NBUF = 3
        E_ = [at(f"soft{i}", 48 + 16 * i, [P, S]) for i in range(NBUF)]
        R_ = [at(f"relu{i}", 52 + 16 * i, [P, S]) for i in range(NBUF)]
        G_ = [at(f"suffix{i}", 56 + 16 * i, [P, S]) for i in range(NBUF)]
        AT_ = [at(f"probsT{i}", 60 + 16 * i, [P, NT, P]) for i in range(NBUF)]
        w_out_sb = at("w_out_sb", 48, [P, 2 * CB, D])
        yT = [at(f"yT{i}", 80 + 4 * i, [P, 2 * CB, P]) for i in range(2)]
        xn2 = [at(f"xn2_{i}", 88 + 4 * i, [P, D]) for i in range(2)]
        xn2T = [at(f"xn2T_{i}", 32 + 4 * i, [P, KT, P]) for i in range(2)]
        g2b = at("g2b", 40, [P, D])
        sq2 = at("sq2", 44, [P, D])

        small = [96 * KIB]

        def keep(name, shape, dt=F32):
            size = 4
            for n in shape[1:]:
                size *= n
            kib = small[0] / KIB
            small[0] += (size + 31) // 32 * 32
            assert small[0] <= 103.5 * KIB
            return at(name, kib, shape, dt)

        ident = keep("ident", [P, P])
        same_head = keep("same_head", [P, P])
        identr = keep("identr", [P, P], F32R)
        maskr = keep("maskr", [P, P], F32R)
        eps = keep("eps", [P, 1])
        ss = keep("ss", [P, 2])
        rt = keep("rt", [P, 2])
        rr = keep("rr", [P, 2])
        gains = keep("gains", [P, 12])
        gain_attn = keep("gain_attn", [P, CB])
        taps = keep("taps", [P, TAPS, CB])
        router_w = keep("router_w", [P, KT, LOG])
        router_b = keep("router_b", [P, LOG])

        u = at("u", 103.5, [P, CB, S + TAPS - 1])
        v = at("v", 103.5, [P, NT, CW])
        big = at("big", 120, [P, 12, S])
        T0 = 168
        xt = [at(f"xt{i}", T0 + 4 * i, [P, D]) for i in range(2)]
        xn = [at(f"xn{i}", T0 + 8 + 4 * i, [P, D]) for i in range(2)]
        g1b = at("g1b", T0 + 16, [P, D])
        sq1 = at("sq1", T0 + 20, [P, D])
        conv = at("conv", T0 + 24, [P, S])
        nsq = [at(f"nsq{i}", T0 + 4 * i, [P, S]) for i in range(2)]
        nrt = [at(f"nrt{i}", T0 + 8 + 4 * i, [P, S]) for i in range(2)]
        q_hi = at("q_hi", T0, [P, S], F32R)
        q_lo = at("q_lo", T0 + 4, [P, S], F32R)
        k_hi = at("k_hi", T0 + 8, [P, S], F32R)
        k_lo = at("k_lo", T0 + 12, [P, S], F32R)
        v_pair = at("v_pair", T0 + 16, [P, NT, P])
        x2 = at("x2", T0, [P, NT, D])
        logits = keep("logits", [P, NT, LOG])

        psf = ps.rearrange("p a b -> p (a b)")

        may_start = sem("may_start")

        def start_step(pool):
            pool.sem_inc(may_start, 1)

        consts_in = sem("consts_in")
        consts_made = sem("consts_made")
        x_landed = [sem(f"x_landed{i}") for i in range(2)]
        x_squared = sem("x_squared")
        x_rooted = sem("x_rooted")
        x_inverse = sem("x_inverse")
        x_scaled = sem("x_scaled")
        x_turned = sem("x_turned")
        x_hi_made = sem("x_hi_made")
        w_landed = [sem(f"w_landed{i}") for i in range(2)]
        w_hi_made = sem("w_hi_made")
        w_lo_made = sem("w_lo_made")
        w_used = sem("w_used")
        banks_filled = sem("banks_filled")
        banks_read = sem("banks_read")
        u_made = sem("u_made")
        conv_step = sem("conv_step")
        router_in = sem("router_in")

        with nc.Block() as block:

            @block.sync
            def _(sp):
                for i in range(2):
                    sp.dma_start(xt[i], xv[i]).then_inc(x_landed[i], 16)
                sp.dma_start(g1b, norm_mix_w.partition_broadcast(P)[:, 0, :]).then_inc(consts_in, 16)
                for h in range(2):
                    rows = slice(h * HD, (h + 1) * HD)
                    sp.dma_start(gains[rows, 4:5], q_norm_w.rearrange("a d -> d a")).then_inc(consts_in, 16)
                    sp.dma_start(gains[rows, 8:9], k_norm_w.rearrange("a d -> d a")).then_inc(consts_in, 16)
                with nc.allow_non_contiguous_dma(reason="small columns"):
                    sp.dma_start(gains[:, 0:4], group_norm_conv_w.rearrange("a (b g) d -> (g d) (a b)", g=2)).then_inc(consts_in, 16)
                    sp.dma_start(gain_attn, group_norm_attn_w.rearrange("a (b g) d -> (g d) (a b)", g=2)).then_inc(consts_in, 16)
                    for j in range(TAPS):
                        sp.dma_start(taps[:, j, :], conv_w[0, j].rearrange("(b p) -> p b", p=P)).then_inc(consts_in, 16)
                for hf in range(2):
                    sp.dma_start(w_raw[hf], w_in_v[:, 4 * hf:4 * hf + 4, 0:CW]).then_inc(w_landed[hf], 16)
                with nc.allow_non_contiguous_dma(reason="small columns"):
                    sp.dma_start(router_w[:, :, 0:NG], w_group.rearrange("a (p k) g -> p (a k) g", k=KT)).then_inc(router_in, 16)
                    sp.dma_start(router_w[:, :, NG:], w_expert.rearrange("a (p k) g -> p (a k) g", k=KT)).then_inc(router_in, 16)
                with sp.Fori(1, NT // 2) as i:
                    for b in range(2):
                        sp.wait_ge(x_scaled, 2 * i + b - 1)
                        sp.dma_start(xt[b], xv[bass.ds(2 * i + b, 1)].rearrange("m p d -> p (m d)")).then_inc(x_landed[b], 16)
                with sp.Fori(1, NCH) as c:
                    for hf in range(2):
                        sp.wait_ge(w_lo_made, 8 * c + 4 * hf - 4)
                        sp.dma_start(w_raw[hf], w_in_v[:, 4 * hf:4 * hf + 4, bass.ds(c * CW, CW)]).then_inc(w_landed[hf], 16)
                sp.dma_start(router_b[:, 0:NG], b_group.partition_broadcast(P)[:, 0, :]).then_inc(router_in, 16)
                sp.dma_start(router_b[:, NG:], b_expert.partition_broadcast(P)[:, 0, :]).then_inc(router_in, 16)
                sp.wait_ge(router_in, 16 * 4)

            @block.gpsimd
            def _(pool):
                pool.memset(ident, 0.0).then_inc(consts_made, 1)
                pool.memset(maskr.bitcast(F32), 0.0).then_inc(consts_made, 1)
                pool.memset(same_head, 0.0).then_inc(consts_made, 1)
                pool.memset(eps, EPS).then_inc(consts_made, 1)
                pool.memset(u[:, :, 0:TAPS - 1], 0.0).then_inc(consts_made, 1)
                pool.wait_ge(consts_made, 5)
                pool.affine_select(out=ident, in_=ident, compare_op=ALU.not_equal, fill=1.0, base=0,
                                   pattern=[[-1, P]], channel_multiplier=1).then_inc(consts_made, 1)
                pool.wait_ge(consts_made, 6)
                pool.memset(same_head[0:HD, 0:HD], 1.0).then_inc(consts_made, 1)
                pool.wait_ge(consts_made, 7)
                pool.memset(same_head[HD:P, HD:P], 1.0).then_inc(consts_made, 1)
                pool.wait_ge(consts_made, 8)
                pool.tensor_copy(identr, ident).then_inc(consts_made, 1)
                pool.affine_select(out=maskr, in_=maskr.bitcast(F32), compare_op=ALU.is_gt, fill=MASKED, base=0,
                                   pattern=[[-1, P]], channel_multiplier=1).then_inc(consts_made, 1)

            @block.scalar
            def _(act):
                act.wait_ge(consts_made, 10)
                with act.Fori(0, NT // 2) as i:
                    for b in range(2):
                        act.wait_ge(x_landed[b], 16 * i + 16)
                        act.activation(sq1, xt[b], ACT.Square, accum_out=ss[:, b:b + 1]).then_inc(x_squared, 1)
                        act.wait_ge(x_squared, 2 * i + b + 1)
                        act.activation(rt[:, b:b + 1], ss[:, b:b + 1], ACT.Sqrt, bias=eps, scale=1.0 / D).then_inc(x_rooted, 1)
                    for b in range(2):
                        act.wait_ge(x_turned, 2 * i + b + 1)
                        act.activation(xnT_hi[:, :, bass.ds((2 * i + b) * P, P)],
                                       psf[:, b * D:(b + 1) * D].rearrange("p (k t) -> p k t", k=KT),
                                       ACT.Copy).then_inc(x_hi_made, 1)

                def split(c, k):
                    if k % 4 == 0:
                        act.wait_ge(w_landed[k // 4], 16 * (c + 1))
                    if k >= 4:
                        act.wait_ge(w_used, 7 * c + k - 3)
                    elif c and k < 3:
                        act.wait_ge(w_used, 7 * (c - 1) + k + 5)
                    elif c:
                        act.wait_ge(banks_filled, 8 * c)
                    act.activation(w_hi[:, k % 4], w_raw[k // 4][:, k % 4], ACT.Copy).then_inc(w_hi_made, 1)

                def empty(c):
                    for b in range(8):
                        act.wait_ge(banks_filled, 8 * c + b + 1)
                        if c == 5:
                            dst = v[:, b, :]
                            if b == 0:
                                act.wait_ge(conv_step, 4 * CB)
                        elif c == 1:
                            h = b % 2
                            dst = u[:, b // 2, TAPS - 1 + h * BANK:TAPS - 1 + (h + 1) * BANK]
                        else:
                            row = {0: 0, 3: 4, 4: 8}[c] + b // 2
                            dst = big[:, row, (b % 2) * BANK:(b % 2 + 1) * BANK]
                        act.activation(dst, ps[:, b], ACT.Copy).then_inc(banks_read, 1)

                for c in range(NCH):
                    for k in range(8):
                        if k == 3 and c and c - 1 != 2:
                            empty(c - 1)
                        split(c, k)
                empty(NCH - 1)

            @block.vector
            def _(dve):
                dve.wait_ge(consts_in, 16 * 10)
                with dve.Fori(0, NT // 2) as i:
                    for b in range(2):
                        dve.wait_ge(x_rooted, 2 * i + b + 1)
                        dve.reciprocal(rr[:, b:b + 1], rt[:, b:b + 1]).then_inc(x_inverse, 1)
                        dve.wait_ge(x_inverse, 2 * i + b + 1)
                        dve.wait_ge(x_turned, 2 * i)
                        dve.scalar_tensor_tensor(xn[b], xt[b], rr[:, b:b + 1], g1b, ALU.mult, ALU.mult).then_inc(x_scaled, 1)
                    for b in range(2):
                        dve.wait_ge(x_hi_made, 2 * i + b + 1)
                        cols = bass.ds((2 * i + b) * P, P)
                        dve.tensor_tensor(xnT_lo[:, :, cols], psf[:, b * D:(b + 1) * D].rearrange("p (k t) -> p k t", k=KT),
                                          xnT_hi[:, :, cols].bitcast(F32), ALU.subtract).then_inc(banks_read, 1)

                def convolve(j):
                    n = 4 * j
                    for tap in range(TAPS):
                        src = u[:, j, tap:tap + S]
                        w = taps[:, tap, j:j + 1]
                        if tap == 0:
                            if j:
                                dve.wait_ge(conv_step, n)
                            dve.tensor_scalar(conv, src, w, None, ALU.mult).then_inc(conv_step, 1)
                        else:
                            dve.wait_ge(conv_step, n + tap)
                            dve.scalar_tensor_tensor(conv, src, w, conv, ALU.mult, ALU.add).then_inc(conv_step, 1)
                    dve.wait_ge(conv_step, n + 3)
                    dve.tensor_tensor(big[:, j], big[:, j], conv, ALU.mult).then_inc(conv_step, 1)

                for c in range(NCH):
                    for k in range(8):
                        if k == 3 and c - 1 == 2:
                            for b in range(8):
                                dve.wait_ge(banks_filled, 8 * (c - 1) + b + 1)
                                dve.wait_ge(banks_read, 8 + 16)
                                h = b % 2
                                dst = u[:, b // 2, TAPS - 1 + h * BANK:TAPS - 1 + (h + 1) * BANK]
                                dve.tensor_tensor(dst, ps[:, b], dst, ALU.mult).then_inc(banks_read, 1)
                            dve.wait_ge(banks_read, 8 + 24)
                        dve.wait_ge(w_hi_made, 8 * c + k + 1)
                        dve.tensor_tensor(w_lo[:, k % 4], w_raw[k // 4][:, k % 4], w_hi[:, k % 4].bitcast(F32),
                                          ALU.subtract).then_inc(w_lo_made, 1)
                        if c == 3 and k >= 4:
                            convolve(k - 4)

            @block.tensor
            def _(pe):
                pe.wait_ge(consts_made, 10)
                with pe.Fori(0, NT // 2) as i:
                    for b in range(2):
                        pe.wait_ge(x_scaled, 2 * i + b + 1)
                        pe.wait_ge(banks_read, 2 * i)
                        for k in range(KT):
                            t = pe.transpose(psf[:, b * D + k * P:b * D + (k + 1) * P], xn[b][:, k:D:KT], ident)
                        t.then_inc(x_turned, 1)
                pe.wait_ge(banks_read, NT)
                THREE = [("hi", "hi"), ("hi", "lo"), ("lo", "hi")]
                with pe.Fori(0, NCH - 1) as c:
                    for k in range(KT):
                        pe.wait_ge(w_lo_made, 8 * c + k + 1)
                        for b in range(8):
                            if k == 0:
                                pe.wait_ge(banks_read, 8 * c + b + 1)
                            for j, (a, z) in enumerate(THREE):
                                w = (w_hi if a == "hi" else w_lo)[:, k % 4, (b // 2) * P:(b // 2 + 1) * P]
                                r = (xnT_hi if z == "hi" else xnT_lo)[:, k, (b % 2) * BANK:(b % 2 + 1) * BANK]
                                mm = pe.matmul(ps[:, b], w, r, start=(k == 0 and j == 0), stop=(k == KT - 1 and j == 2))
                            if k == KT - 1:
                                mm.then_inc(banks_filled, 1)
                        if k < KT - 1:
                            mm.then_inc(w_used, 1)
                c = NCH - 1
                for k in range(KT):
                    pe.wait_ge(w_lo_made, 8 * c + k + 1)
                    for b in range(8):
                        if k == 0:
                            pe.wait_ge(banks_read, 8 * c + b + 1)
                        for j, (a, z) in enumerate(THREE):
                            w = (w_hi if a == "hi" else w_lo)[:, k % 4]
                            r = (xnT_hi if z == "hi" else xnT_lo)[:, k, b * P:(b + 1) * P]
                            mm = pe.matmul(ps[:, b], r, w, start=(k == 0 and j == 0), stop=(k == KT - 1 and j == 2))
                        if k == KT - 1:
                            mm.then_inc(banks_filled, 1)
                    if k < KT - 1:
                        mm.then_inc(w_used, 1)

        def norm_sems(tag):
            return {n: sem(f"{tag}_{n}") for n in ("squared", "summed", "rooted", "inverted", "scaled")}

        def norm_scalar(act, s, n, row):
            with act.Fori(0, n) as i:
                for b in range(2):
                    act.wait_ge(s["summed"], 4 * i)
                    act.activation(nsq[b], big[:, bass.ds(2 * i + b + row, 1)].rearrange("p a t -> p (a t)"),
                                   ACT.Square).then_inc(s["squared"], 1)
                for b in range(2):
                    act.wait_ge(s["summed"], 4 * i + 2 * b + 2)
                    act.wait_ge(s["scaled"], 2 * i)
                    act.activation(nrt[b], psf[:, b * S:(b + 1) * S], ACT.Sqrt, bias=eps, scale=1.0 / HD).then_inc(s["rooted"], 1)

        def norm_tensor(pe, s, n):
            with pe.Fori(0, n) as i:
                for b in range(2):
                    pe.wait_ge(s["squared"], 2 * i + b + 1)
                    pe.wait_ge(s["rooted"], 2 * i)
                    for h in range(2):
                        pe.matmul(ps[:, 2 * b + h], same_head, nsq[b][:, h * BANK:(h + 1) * BANK],
                                  start=True, stop=True).then_inc(s["summed"], 1)

        def norm_vector(dve, s, n, row, gain):
            with dve.Fori(0, n) as i:
                for b in range(2):
                    blk = big[:, bass.ds(2 * i + b + row, 1)].rearrange("p a t -> p (a t)")
                    dve.wait_ge(s["rooted"], 2 * i + b + 1)
                    dve.reciprocal(nrt[b], nrt[b]).then_inc(s["inverted"], 1)
                    dve.wait_ge(s["inverted"], 2 * i + b + 1)
                    dve.scalar_tensor_tensor(blk, blk, gain[:, bass.ds(2 * i + b, 1)], nrt[b],
                                             ALU.mult, ALU.mult).then_inc(s["scaled"], 1)

        s_n1 = norm_sems("norm1")
        gains_made = sem("gains_made")
        with nc.Block() as block:

            @block.scalar
            def _(act):
                norm_scalar(act, s_n1, 6, 0)

            @block.tensor
            def _(pe):
                norm_tensor(pe, s_n1, 6)

            @block.vector
            def _(dve):
                dve.tensor_scalar(gains[:, 4:5], gains[:, 4:5], float(HD) ** -0.5, None, ALU.mult).then_inc(gains_made, 1)
                dve.wait_ge(gains_made, 1)
                for j in range(1, CB):
                    dve.tensor_copy(gains[:, 4 + j:5 + j], gains[:, 4:5]).then_inc(gains_made, 1)
                    dve.tensor_copy(gains[:, 8 + j:9 + j], gains[:, 8:9]).then_inc(gains_made, 1)
                dve.wait_ge(gains_made, 2 * CB - 1)
                norm_vector(dve, s_n1, 6, 0, gains)

        UNITS = 2 * NT
        staged = sem("staged")
        scored = sem("scored")
        absolute = sem("absolute")
        small_exp = sem("small_exp")
        small_ln = sem("small_ln")
        relued = sem("relued")
        summed = sem("summed")
        logged = sem("logged")
        weighed = sem("weighed")
        turned = sem("turned")
        turned_read = sem("turned_read")
        valued = sem("valued")
        out_read = sem("out_read")
        w_in_e = {}
        L = lambda n: (n // 2 + 1) * P
        TH = sum((L(n) + BANK - 1) // BANK for n in range(UNITS))
        th_before = [sum((L(m) + BANK - 1) // BANK for m in range(n)) for n in range(UNITS + 1)]
        ZB = lambda n: psf[:, (n % NBUF) * S:(n % NBUF) * S + L(n)]
        expert_w = [[sem(f"expert_w{m}_{i}") for m in (1, 3, 2)] for i in range(2)]

        with nc.Block() as block:

            @block.sync
            def _(sp):
                sp.dma_start(W1[0], w1_v[0]).then_inc(expert_w[0][0], 16)
                sp.dma_start(W3[0], w3_v[0]).then_inc(expert_w[0][1], 16)

            @block.gpsimd
            def _(pool):
                with pool.Fori(0, CB) as p:
                    flat = lambda a: a.rearrange("p a t -> p (a t)")
                    q = flat(big[:, bass.ds(p + 4, 1)])
                    k = flat(big[:, bass.ds(p + 8, 1)])
                    pool.wait_ge(scored, UNITS * p)
                    pool.tensor_copy(q_hi, q).then_inc(staged, 1)
                    pool.tensor_copy(k_hi, k).then_inc(staged, 1)
                    pool.wait_ge(staged, 5 * p + 2)
                    start_step(pool)
                    pool.tensor_tensor(q_lo, q, q_hi.bitcast(F32), ALU.subtract).then_inc(staged, 1)
                    pool.tensor_tensor(k_lo, k, k_hi.bitcast(F32), ALU.subtract).then_inc(staged, 1)
                    pool.wait_ge(valued, UNITS * p)
                    pool.tensor_copy(v_pair, v[:, :, bass.ds(p * P, P)]).then_inc(staged, 1)

            @block.tensor
            def _(pe):
                def scores(p, n):
                    t, h = n // 2, n % 2
                    rows = slice(h * HD, (h + 1) * HD)
                    if n == 0:
                        pe.wait_ge(staged, 5 * p + 4)
                    if n >= NBUF:
                        pe.wait_ge(logged, UNITS * p + n - NBUF + 1)
                    else:
                        pe.wait_ge(logged, UNITS * p)
                    z = ZB(n)
                    for c0 in range(0, L(n), BANK):
                        c1 = min(c0 + BANK, L(n))
                        last = c1 == L(n)
                        cols = slice(t * P, (t + 1) * P)
                        pe.matmul(z[:, c0:c1], q_hi[rows, cols], k_hi[rows, c0:c1], start=True, stop=False)
                        pe.matmul(z[:, c0:c1], q_hi[rows, cols], k_lo[rows, c0:c1], start=False, stop=False)
                        mm = pe.matmul(z[:, c0:c1], q_lo[rows, cols], k_hi[rows, c0:c1], start=False, stop=not last)
                    mm = pe.matmul(z[:, L(n) - P:L(n)], identr, maskr, start=False, stop=True)
                    mm.then_inc(scored, 1)

                def turn(p, n, half):
                    g = th_before[n] + half
                    if half == 0:
                        pe.wait_ge(weighed, UNITS * p + n + 1)
                    pe.wait_ge(turned_read, TH * p + g)
                    for j in range(4 * half, min(4 * half + 4, L(n) // P)):
                        mm = pe.transpose(ps[:, 6, (j % 4) * P:(j % 4 + 1) * P], G_[n % NBUF][:, j * P:(j + 1) * P], ident)
                    mm.then_inc(turned, 1)

                def values(p, n):
                    t, h = n // 2, n % 2
                    if n == 0:
                        pe.wait_ge(staged, 5 * p + 5)
                    pe.wait_ge(turned_read, TH * p + th_before[n + 1])
                    if n % 8 == 0:
                        pe.wait_ge(out_read, 2 * p + n // 8)
                    for j in range(t + 1):
                        mm = pe.matmul(ps[h * HD:(h + 1) * HD, 7, (t % 4) * P:(t % 4 + 1) * P],
                                       v_pair[:, j, h * HD:(h + 1) * HD], AT_[n % NBUF][:, j, :],
                                       start=(j == 0), stop=(j == t))
                    mm.then_inc(valued, 1)

                with pe.Fori(0, CB) as p:
                    scores(p, 0)
                    scores(p, 1)
                    for n in range(UNITS + 3):
                        if n + 2 < UNITS:
                            scores(p, n + 2)
                        if 1 <= n <= UNITS:
                            turn(p, n - 1, 0)
                        if 3 <= n:
                            values(p, n - 3)
                        if 1 <= n <= UNITS and L(n - 1) > BANK:
                            turn(p, n - 1, 1)

            @block.scalar
            def _(act):
                def step(p, n):
                    if n + 1 < UNITS:
                        m = n + 1
                        act.wait_ge(scored, UNITS * p + m + 1)
                        if m >= NBUF:
                            act.wait_ge(logged, UNITS * p + m - NBUF + 1)
                        else:
                            act.wait_ge(logged, UNITS * p)
                        act.activation(E_[m % NBUF][:, :L(m)], ZB(m), ACT.Abs).then_inc(absolute, 1)
                    if n >= 0 and n < UNITS:
                        act.wait_ge(small_exp, UNITS * p + n + 1)
                        e = E_[n % NBUF][:, :L(n)]
                        act.activation(e, e, ACT.Ln, bias=1.0).then_inc(small_ln, 1)
                    if 1 <= n:
                        act.wait_ge(logged, UNITS * p + n)
                        g = G_[(n - 1) % NBUF][:, :L(n - 1)]
                        act.activation(g, g, ACT.Exp).then_inc(weighed, 1)
                    if n + 1 < UNITS:
                        m = n + 1
                        act.wait_ge(absolute, UNITS * p + m + 1)
                        e = E_[m % NBUF][:, :L(m)]
                        act.activation(e, e, ACT.Exp, scale=-1.0).then_inc(small_exp, 1)

                with act.Fori(0, CB) as p:
                    for n in range(-1, UNITS + 1):
                        step(p, n)
                        if n == 10 or n == UNITS:
                            hf = 0 if n == 10 else 1
                            act.wait_ge(valued, UNITS * p + 8 * (hf + 1))
                            act.activation(big[:, bass.ds(p + 4, 1), hf * BANK:(hf + 1) * BANK].rearrange("p a t -> p (a t)"),
                                           ps[:, 7], ACT.Copy).then_inc(out_read, 1)

            @block.vector
            def _(dve):
                def step(p, n):
                    if n + 1 < UNITS:
                        m = n + 1
                        dve.wait_ge(absolute, UNITS * p + m + 1)
                        dve.tensor_scalar(R_[m % NBUF][:, :L(m)], ZB(m), 0.0, None, ALU.max).then_inc(relued, 1)
                    if 0 <= n < UNITS:
                        dve.wait_ge(small_ln, UNITS * p + n + 1)
                        dve.wait_ge(relued, UNITS * p + n + 1)
                        if n >= NBUF:
                            dve.wait_ge(turned, TH * p + th_before[n - NBUF + 1])
                        else:
                            dve.wait_ge(turned, TH * p)
                        l = L(n)
                        g, e, r = (b[n % NBUF][:, l - 1::-1] if l == S else b[n % NBUF][:, l - 1::-1] for b in (G_, E_, R_))
                        dve.tensor_tensor_scan(g, e, r, 0.0, ALU.add, ALU.add).then_inc(summed, 1)
                    if 2 <= n:
                        m = n - 2
                        for hf in range(th_before[m + 1] - th_before[m]):
                            dve.wait_ge(turned, TH * p + th_before[m] + hf + 1)
                            if hf == 0:
                                dve.wait_ge(valued, UNITS * p + max(m - NBUF + 1, 0))
                            k0, k1 = 4 * hf, min(4 * hf + 4, L(m) // P)
                            dve.tensor_copy(AT_[m % NBUF][:, k0:k1, :],
                                            ps[:, 6, 0:(k1 - k0) * P].rearrange("p (k t) -> p k t", t=P)).then_inc(turned_read, 1)
                    if 0 <= n < UNITS:
                        dve.wait_ge(summed, UNITS * p + n + 1)
                        g = G_[n % NBUF][:, :L(n)]
                        dve.tensor_tensor(g, ZB(n), g, ALU.subtract).then_inc(logged, 1)

                with dve.Fori(0, CB) as p:
                    for n in range(-1, UNITS + 2):
                        step(p, n)

        s_n2 = norm_sems("norm2")
        w_out_in = sem("w_out_in")
        with nc.Block() as block:

            @block.sync
            def _(sp):
                sp.dma_start(w_out_sb, w_out_v).then_inc(w_out_in, 16)

            @block.scalar
            def _(act):
                norm_scalar(act, s_n2, CB // 2, CB)

            @block.tensor
            def _(pe):
                norm_tensor(pe, s_n2, CB // 2)

            @block.vector
            def _(dve):
                norm_vector(dve, s_n2, CB // 2, CB, gain_attn)

        x_in = sem("x_in")
        g2_in = sem("g2_in")
        y_staged = sem("y_staged")
        mixed = sem("mixed")
        x2_made = sem("x2_made")
        x2_squared = sem("x2_squared")
        x2_rooted = sem("x2_rooted")
        x2_inverse = sem("x2_inverse")
        xn2_made = sem("xn2_made")
        xn2_turned = sem("xn2_turned")
        xn2T_made = sem("xn2T_made")
        logits_summed = sem("logits_summed")
        logits_made = sem("logits_made")
        xn2_stored = [sem(f"xn2_stored{i}") for i in range(2)]
        xn2_rows_v = xn2_rows.rearrange("(m p) d -> m p d", p=P)
        x_all = x.rearrange("a (m p) d -> p (a m) d", p=P)
        one = lambda a: a.rearrange("p a d -> p (a d)")

        with nc.Block() as block:

            @block.sync
            def _(sp):
                sp.dma_start(x2, x_all).then_inc(x_in, 16)
                sp.dma_start(g2b, norm_ffn_w.partition_broadcast(P)[:, 0, :]).then_inc(g2_in, 16)
                with sp.Fori(0, NT // 2) as i:
                    for b in range(2):
                        sp.wait_ge(xn2_made, 2 * i + b + 1)
                        sp.dma_start(xn2_rows_v[bass.ds(2 * i + b, 1)].rearrange("m p d -> p (m d)"), xn2[b]).then_inc(xn2_stored[b], 16)
                for b in range(2):
                    sp.wait_ge(xn2_stored[b], 16 * (NT // 2))

            @block.gpsimd
            def _(pool):
                with pool.Fori(0, NT // 2) as i:
                    for b in range(2):
                        pool.wait_ge(mixed, 4 * i)
                        pool.tensor_copy(yT[b], big[:, 0:2 * CB, bass.ds((2 * i + b) * P, P)]).then_inc(y_staged, 1)

            @block.tensor
            def _(pe):
                pe.wait_ge(w_out_in, 16)

                def multiply(m, b):
                    pe.wait_ge(y_staged, m + 1)
                    for h in range(2):
                        if not (isinstance(m, int) and m < 2):
                            pe.wait_ge(x2_made, 2 * m + h - 3)
                        for c in range(2 * CB):
                            mm = pe.matmul(ps[:, 2 * b + h], yT[b][:, c], w_out_sb[:, c, h * BANK:(h + 1) * BANK],
                                           start=(c == 0), stop=(c == 2 * CB - 1))
                        mm.then_inc(mixed, 1)

                def route(m, b):
                    pe.wait_ge(xn2_made, m + 1)
                    pe.wait_ge(xn2T_made, m)
                    for k in range(KT):
                        mm = pe.transpose(psf[:, 4 * BANK + k * P:4 * BANK + (k + 1) * P], xn2[b][:, k:D:KT], ident)
                    mm.then_inc(xn2_turned, 1)
                    pe.wait_ge(xn2T_made, m + 1)
                    if not (isinstance(m, int) and m < 2):
                        pe.wait_ge(logits_made, m - 1)
                    for k in range(KT):
                        mm = pe.matmul(ps[:, 6 + b, 0:LOG], xn2T[b][:, k], router_w[:, k], start=(k == 0), stop=(k == KT - 1))
                    mm.then_inc(logits_summed, 1)

                multiply(0, 0)
                multiply(1, 1)
                route(0, 0)
                with pe.Fori(1, NT // 2) as i:
                    multiply(2 * i, 0)
                    route(2 * i - 1, 1)
                    multiply(2 * i + 1, 1)
                    route(2 * i, 0)
                route(NT - 1, 1)

            @block.scalar
            def _(act):
                def turned_out(m, b):
                    act.wait_ge(xn2_turned, m + 1)
                    if not (isinstance(m, int) and m < 2):
                        act.wait_ge(logits_summed, m - 1)
                    act.activation(xn2T[b].rearrange("p k t -> p (k t)"), psf[:, 4 * BANK:6 * BANK], ACT.Copy).then_inc(xn2T_made, 1)

                def square(m, b):
                    act.wait_ge(x2_made, 2 * m + 2)
                    act.activation(sq2, one(x2[:, bass.ds(m, 1)]), ACT.Square, accum_out=ss[:, b:b + 1]).then_inc(x2_squared, 1)
                    act.wait_ge(x2_squared, m + 1)
                    act.activation(rt[:, b:b + 1], ss[:, b:b + 1], ACT.Sqrt, bias=eps, scale=1.0 / D).then_inc(x2_rooted, 1)

                square(0, 0)
                square(1, 1)
                turned_out(0, 0)
                with act.Fori(1, NT // 2) as i:
                    square(2 * i, 0)
                    turned_out(2 * i - 1, 1)
                    square(2 * i + 1, 1)
                    turned_out(2 * i, 0)
                turned_out(NT - 1, 1)

            @block.vector
            def _(dve):
                dve.wait_ge(x_in, 16)
                dve.wait_ge(g2_in, 16)
                dve.wait_ge(router_in, 64)

                def add(m, b):
                    for h in range(2):
                        dve.wait_ge(mixed, 2 * m + h + 1)
                        half = one(x2[:, bass.ds(m, 1), h * BANK:(h + 1) * BANK])
                        dve.tensor_tensor(half, ps[:, 2 * b + h], half, ALU.add).then_inc(x2_made, 1)
                    dve.wait_ge(x2_rooted, m + 1)
                    dve.reciprocal(rr[:, b:b + 1], rt[:, b:b + 1]).then_inc(x2_inverse, 1)
                    dve.wait_ge(x2_inverse, m + 1)
                    if not (isinstance(m, int) and m < 2):
                        dve.wait_ge(xn2_turned, m - 1)
                        dve.wait_ge(xn2_stored[b], (m // 2) * 16 if isinstance(m, int) else (m - b) * 8)
                    dve.scalar_tensor_tensor(xn2[b], one(x2[:, bass.ds(m, 1)]), rr[:, b:b + 1], g2b, ALU.mult, ALU.mult).then_inc(xn2_made, 1)

                def bias(m, b):
                    dve.wait_ge(logits_summed, m + 1)
                    dve.tensor_tensor(one(logits[:, bass.ds(m, 1)]), ps[:, 6 + b, 0:LOG], router_b, ALU.add).then_inc(logits_made, 1)

                add(0, 0)
                add(1, 1)
                bias(0, 0)
                with dve.Fori(1, NT // 2) as i:
                    add(2 * i, 0)
                    bias(2 * i - 1, 1)
                    add(2 * i + 1, 1)
                    bias(2 * i, 0)
                bias(NT - 1, 1)

        room = [int(103.5 * KIB)]

        def place(name, shape, dt=F32):
            size = 4
            for n in shape[1:]:
                size *= n
            kib = room[0] / KIB
            room[0] += (size + 31) // 32 * 32
            assert room[0] <= T0 * KIB
            return at(name, kib, shape, dt)

        COLS = NBLK * NE
        iota = place("iota", [P, COLS])
        iota_p1 = place("iota_p1", [P, 1])
        pair_code = [place(f"pair_code{k}", [P, NT]) for k in range(2)]
        past = place("past", [P, NBLK - 1, NE])
        before = place("before", [P, P], BF16)
        ones = place("ones", [P, P], BF16)
        d4 = place("d4", [P, NT, NG])
        e4 = place("e4", [P, NT, NG])
        c4 = place("c4", [P, NT, NG])
        of_group = place("of_group", [P, NT, NG])
        picked = place("picked", [P, NT, NG, EPG])
        sel = [place(f"sel{k}", [P, NT, EPG]) for k in range(2)]
        c8 = place("c8", [P, NT, EPG])
        of_choice = place("of_choice", [P, NT, EPG])
        top = [place(f"top{k}", [P, NT]) for k in range(3)]
        which = [place(f"which{k}", [P, NT]) for k in range(3)]
        e_diff = place("e_diff", [P, NT])
        p_group = place("p_group", [P, NT])
        gate = [keep(f"gate{k}", [P, NT]) for k in range(2)]
        expert = [place(f"expert{k}", [P, NT]) for k in range(2)]
        of_expert = [place(f"of_expert{k}", [P, NT, NE]) for k in range(2)]
        chosen = place("chosen", [P, NT, NE], BF16)
        ranked = place("ranked", [P, NT, NE])
        rank = [place(f"rank{k}", [P, NT]) for k in range(2)]
        rank_i = place("rank_i", [P, NT], I32)
        part_i = place("part_i", [P, NT], I32)
        column = [place(f"column{k}", [P, NT]) for k in range(2)]
        slot = [place(f"slot{k}", [P, NT]) for k in range(2)]
        NOH = 4
        of_slot = [place(f"of_slot{i}", [P, P], F32R) for i in range(NOH)]
        of_column = [place(f"of_column{i}", [P, COLS], F32R) for i in range(NOH)]
        unused = place("unused", [P, COLS])
        pair_f = place("pair_f", [P, COLS])
        over = place("over", [P, NBLK - 1, NE])
        over_at = place("over_at", [P, (NBLK - 1) * NE])
        over_sel = place("over_sel", [P, (NBLK - 1) * NE])
        over_col = place("over_col", [P, 1])
        slot_pair = keep("slot_pair", [P, COLS], I32)
        slot_token = keep("slot_token", [P, COLS], I32)
        over_list = keep("over_list", [1, OVER + 1], I32)
        over_n = keep("over_n", [1, 1], I32)

        iotas = sem("iotas")
        choosing = sem("choosing")
        group_exp = sem("group_exp")
        diff_exp = sem("diff_exp")
        counted = sem("counted")
        hot = sem("hot")
        table_step = sem("table_step")
        listed = sem("listed")

        with nc.Block() as block:

            @block.sync
            def _(sp):
                sp.dma_start(W2[0], w2_v[0]).then_inc(expert_w[0][2], 16)
                sp.dma_start(W1[1], w1_v[1]).then_inc(expert_w[1][0], 16)
                sp.dma_start(W3[1], w3_v[1]).then_inc(expert_w[1][1], 16)
                sp.dma_start(W2[1], w2_v[1]).then_inc(expert_w[1][2], 16)

            @block.gpsimd
            def _(pool):
                small_ints = dict(allow_small_or_imprecise_dtypes=True)
                pool.iota(iota, [[1, COLS]], base=0, channel_multiplier=0, **small_ints).then_inc(iotas, 1)
                pool.iota(iota_p1, [[1, 1]], base=1, channel_multiplier=1, **small_ints).then_inc(iotas, 1)
                for k in range(2):
                    pool.iota(pair_code[k], [[2 * P, NT]], base=1 + k, channel_multiplier=2, **small_ints).then_inc(iotas, 1)
                pool.iota(past, [[P, NBLK - 1], [0, NE]], base=P, channel_multiplier=0, **small_ints).then_inc(iotas, 1)
                pool.memset(ones, 1.0).then_inc(iotas, 1)
                pool.wait_ge(iotas, 6)
                pool.affine_select(out=before, in_=ones, compare_op=ALU.is_gt, fill=0.0, base=0,
                                   pattern=[[1, P]], channel_multiplier=-1).then_inc(iotas, 1)

            @block.scalar
            def _(act):
                act.wait_ge(choosing, 2)
                act.activation(e4, d4, ACT.Exp).then_inc(group_exp, 1)
                act.wait_ge(choosing, 19)
                act.activation(e_diff, e_diff, ACT.Exp).then_inc(diff_exp, 1)

            @block.tensor
            def _(pe):
                pe.wait_ge(iotas, 7)
                pe.wait_ge(choosing, 28)
                for m in range(NT):
                    pe.matmul(ps[:, 0, m * NE:(m + 1) * NE], before, chosen[:, m], start=True, stop=(m == 0))
                    for j in range(m):
                        pe.matmul(ps[:, 0, m * NE:(m + 1) * NE], ones, chosen[:, j], start=False, stop=(j == m - 1))
                for j in range(NT):
                    mm = pe.matmul(ps[:, 1, 0:NE], ones, chosen[:, j], start=(j == 0), stop=(j == NT - 1))
                mm.then_inc(counted, 1)
                for n in range(PAIRS // P):
                    pe.wait_ge(hot, 2 * n + 2)
                    pe.matmul(ps[:, 2, 0:COLS], of_slot[n % NOH], of_column[n % NOH],
                              start=(n == 0), stop=(n == PAIRS // P - 1)).then_inc(table_step, 1)
                pe.wait_ge(listed, 1)
                pe.matmul(ps[0:1, 3, 0:P], over_col, ident, start=True, stop=True).then_inc(table_step, 1)

            @block.vector
            def _(dve):
                done = [0]

                def link(ins):
                    done[0] += 1
                    ins.then_inc(choosing, 1)
                    dve.wait_ge(choosing, done[0])

                wide = lambda a, n: a.unsqueeze(2).to_broadcast([P, NT, n])
                tall = lambda n: iota[:, 0:n].unsqueeze(1).to_broadcast([P, NT, n])

                def first_max(src, n, tmp, largest, index):
                    link(dve.tensor_tensor(tmp, src, wide(largest, n), ALU.is_equal))
                    link(dve.scalar_tensor_tensor(tmp, tmp, -float(COLS), tall(n), ALU.mult, ALU.add))
                    link(dve.tensor_reduce(index, tmp, AX.X, ALU.min))
                    link(dve.tensor_scalar(index, index, float(COLS), None, ALU.add))

                dve.wait_ge(iotas, 7)
                g = logits[:, :, 0:NG]
                link(dve.tensor_reduce(top[0], g, AX.X, ALU.max))
                link(dve.tensor_tensor(d4, g, wide(top[0], NG), ALU.subtract))
                first_max(g, NG, c4, top[0], which[0])
                link(dve.tensor_tensor(of_group, tall(NG), wide(which[0], NG), ALU.is_equal))
                link(dve.tensor_tensor(picked, logits[:, :, NG:].rearrange("p m (g e) -> p m g e", e=EPG),
                                       of_group.unsqueeze(3).to_broadcast([P, NT, NG, EPG]), ALU.mult))
                link(dve.tensor_reduce(sel[0], picked.rearrange("p m g e -> p m e g"), AX.X, ALU.add))
                link(dve.tensor_reduce(top[1], sel[0], AX.X, ALU.max))
                first_max(sel[0], EPG, c8, top[1], which[1])
                link(dve.tensor_tensor(of_choice, tall(EPG), wide(which[1], EPG), ALU.is_equal))
                link(dve.scalar_tensor_tensor(sel[1], of_choice, MASKED, sel[0], ALU.mult, ALU.add))
                link(dve.tensor_reduce(top[2], sel[1], AX.X, ALU.max))
                dve.wait_ge(group_exp, 1)
                link(dve.tensor_reduce(p_group, e4, AX.X, ALU.add))
                link(dve.tensor_tensor(e_diff, top[2], top[1], ALU.subtract))
                first_max(sel[1], EPG, c8, top[2], which[2])
                for k in range(2):
                    link(dve.scalar_tensor_tensor(expert[k], which[0], float(EPG), which[1 + k], ALU.mult, ALU.add))
                    link(dve.tensor_tensor(of_expert[k], tall(NE), wide(expert[k], NE), ALU.is_equal))
                link(dve.tensor_tensor(chosen, of_expert[0], of_expert[1], ALU.add))
                dve.wait_ge(diff_exp, 1)
                link(dve.scalar_tensor_tensor(gate[0], e_diff, 1.0, p_group, ALU.add, ALU.mult))
                link(dve.reciprocal(gate[0], gate[0]))
                link(dve.tensor_tensor(gate[1], gate[0], e_diff, ALU.mult))
                dve.wait_ge(counted, 1)
                for k in range(2):
                    link(dve.tensor_tensor(ranked, ps[:, 0, 0:NT * NE].rearrange("p (m e) -> p m e", e=NE), of_expert[k], ALU.mult))
                    link(dve.tensor_reduce(rank[k], ranked, AX.X, ALU.add))
                    link(dve.tensor_copy(rank_i, rank[k]))
                    link(dve.tensor_scalar(part_i, rank_i, 7, None, ALU.arith_shift_right))
                    link(dve.tensor_copy(column[k], part_i))
                    link(dve.scalar_tensor_tensor(column[k], column[k], float(NE), expert[k], ALU.mult, ALU.add))
                    link(dve.tensor_scalar(part_i, rank_i, P - 1, None, ALU.bitwise_and))
                    link(dve.tensor_copy(slot[k], part_i))
                for n in range(PAIRS // P):
                    k, m = n % 2, n // 2
                    if n >= NOH:
                        dve.wait_ge(table_step, n - NOH + 1)
                    dve.tensor_scalar(of_slot[n % NOH], iota[:, 0:P], slot[k][:, m:m + 1], None, ALU.is_equal).then_inc(hot, 1)
                    dve.tensor_scalar(of_column[n % NOH], iota, column[k][:, m:m + 1], pair_code[k][:, m:m + 1],
                                      ALU.is_equal, ALU.mult).then_inc(hot, 1)
                link(dve.tensor_tensor(over, ps[:, 1, 0:NE].unsqueeze(1).to_broadcast([P, NBLK - 1, NE]), past, ALU.is_gt))
                flags = over.rearrange("p b e -> p (b e)")
                link(dve.tensor_tensor_scan(over_at, flags, flags, 0.0, ALU.add, ALU.max))
                link(dve.scalar_tensor_tensor(over_sel, over_at, iota_p1, flags, ALU.is_equal, ALU.mult))
                link(dve.tensor_tensor(over_sel, over_sel, iota[:, NE:COLS], ALU.mult))
                dve.tensor_reduce(over_col, over_sel, AX.X, ALU.add).then_inc(listed, 1)
                link(dve.tensor_copy(over_n, over_at[0:1, (NBLK - 1) * NE - 1:(NBLK - 1) * NE]))
                dve.wait_ge(table_step, PAIRS // P)
                tab = ps[:, 2, 0:COLS]
                link(dve.tensor_scalar(unused, tab, 0.0, 4.0 * PAIRS, ALU.is_equal, ALU.mult))
                link(dve.scalar_tensor_tensor(pair_f, tab, -1.0, unused, ALU.add, ALU.add))
                link(dve.tensor_copy(slot_pair, pair_f))
                link(dve.tensor_scalar(slot_token, slot_pair, 1, None, ALU.arith_shift_right))
                dve.wait_ge(table_step, PAIRS // P + 1)
                link(dve.tensor_copy(over_list, ps[0:1, 3, 0:OVER + 1]))

        idx_token = [place(f"idx_token{i}", [P, 1], I32) for i in range(2)]
        idx_pair = [place(f"idx_pair{i}", [P, 1], I32) for i in range(2)]
        xg = [place(f"xg{i}", [P, D]) for i in range(2)]
        xT = [place(f"xT{i}", [P, KT, P]) for i in range(2)]
        act_out = [place(f"act_out{i}", [P, F]) for i in range(2)]
        hid = [place(f"hid{i}", [P, F]) for i in range(2)]
        hidT = [place(f"hidT{i}", [P, FT, P]) for i in range(2)]
        y = [place(f"y{i}", [P, D]) for i in range(2)]

        def expert_sems(tag):
            return {n: sem(f"{tag}_{n}") for n in
                    ("tokens_ready", "pairs_ready", "turned", "xT_made", "gated", "upped", "silu", "hidden", "hid_turned", "hidT_made",
                     "downed", "y_made")} | {
                "gathered": [sem(f"{tag}_gathered{i}") for i in range(2)],
                "scattered": [sem(f"{tag}_scattered{i}") for i in range(2)]}

        def pe_turn_x(pe, s, n, b, rounds):
            pe.wait_ge(s["gathered"][b], 16 * rounds)
            pe.wait_ge(s["xT_made"], n)
            for k in range(KT):
                mm = pe.transpose(psf[:, k * P:(k + 1) * P], xg[b][:, k:D:KT], ident)
            mm.then_inc(s["turned"], 1)

        def pe_gate(pe, s, n, b):
            pe.wait_ge(s["xT_made"], n + 1)
            pe.wait_ge(s["silu"], n)
            for k in range(KT):
                mm = pe.matmul(ps[:, 2], xT[b][:, k], W1[b][:, k], start=(k == 0), stop=(k == KT - 1))
            mm.then_inc(s["gated"], 1)

        def pe_up(pe, s, n, b):
            pe.wait_ge(s["hidden"], n)
            for k in range(KT):
                mm = pe.matmul(ps[:, 3], xT[b][:, k], W3[b][:, k], start=(k == 0), stop=(k == KT - 1))
            mm.then_inc(s["upped"], 1)

        def pe_turn_hid(pe, s, n, b):
            pe.wait_ge(s["hidden"], n + 1)
            pe.wait_ge(s["hidT_made"], n)
            for k in range(FT):
                mm = pe.transpose(ps[:, 4, k * P:(k + 1) * P], hid[b][:, k:F:FT], ident)
            mm.then_inc(s["hid_turned"], 1)

        def pe_down(pe, s, n, b):
            pe.wait_ge(s["hidT_made"], n + 1)
            pe.wait_ge(s["y_made"], n)
            for h in range(2):
                for k in range(FT):
                    mm = pe.matmul(ps[:, 5 + h], hidT[b][:, k], W2[b][:, k, h * BANK:(h + 1) * BANK],
                                   start=(k == 0), stop=(k == FT - 1))
            mm.then_inc(s["downed"], 1)

        def act_xT(act, s, n, b):
            act.wait_ge(s["turned"], n + 1)
            act.wait_ge(s["upped"], n)
            act.activation(xT[b].rearrange("p k t -> p (k t)"), psf[:, 0:D], ACT.Copy).then_inc(s["xT_made"], 1)

        def act_silu(act, s, n, b):
            act.wait_ge(s["gated"], n + 1)
            act.wait_ge(s["hidden"], n)
            act.activation(act_out[b], ps[:, 2], ACT.Silu).then_inc(s["silu"], 1)

        def act_y(act, s, n, b, rounds):
            act.wait_ge(s["downed"], n + 1)
            act.wait_ge(s["scattered"][b], 16 * rounds)
            act.activation(y[b], psf[:, 5 * BANK:7 * BANK], ACT.Copy).then_inc(s["y_made"], 1)

        def dve_tokens(dve, s, n, b, col, rounds):
            dve.wait_ge(s["gathered"][b], 16 * rounds)
            dve.tensor_copy(idx_token[b], slot_token[:, bass.ds(col, 1)]).then_inc(s["tokens_ready"], 1)

        def dve_pairs(dve, s, n, b, col, rounds):
            dve.wait_ge(s["scattered"][b], 16 * rounds)
            dve.tensor_copy(idx_pair[b], slot_pair[:, bass.ds(col, 1)]).then_inc(s["pairs_ready"], 1)

        def dve_hid(dve, s, n, b):
            dve.wait_ge(s["upped"], n + 1)
            dve.wait_ge(s["silu"], n + 1)
            dve.wait_ge(s["hid_turned"], n)
            dve.tensor_tensor(hid[b], ps[:, 3], act_out[b], ALU.mult).then_inc(s["hidden"], 1)

        def dve_hidT(dve, s, n, b):
            dve.wait_ge(s["hid_turned"], n + 1)
            dve.wait_ge(s["downed"], n)
            dve.tensor_copy(hidT[b].rearrange("p k t -> p (k t)"), ps[:, 4]).then_inc(s["hidT_made"], 1)

        def pool_gather(pool, s, n, b, turned):
            pool.wait_ge(s["tokens_ready"], n + 1)
            pool.wait_ge(s["turned"], turned)
            start_step(pool)
            pool.indirect_dma_start(out=xg[b], out_offset=None, in_=xn2_rows,
                                    in_offset=bass.IndirectOffsetOnAxis(ap=idx_token[b].bitcast(U32), axis=0),
                                    bounds_check=S - 1, oob_is_err=False).then_inc(s["gathered"][b], 16)

        def pool_scatter(pool, s, n, b):
            pool.wait_ge(s["y_made"], n + 1)
            pool.wait_ge(s["pairs_ready"], n + 1)
            start_step(pool)
            pool.indirect_dma_start(out=y_rows, out_offset=bass.IndirectOffsetOnAxis(ap=idx_pair[b].bitcast(U32), axis=0),
                                    in_=y[b], in_offset=None,
                                    bounds_check=PAIRS - 1, oob_is_err=False).then_inc(s["scattered"][b], 16)

        s_e = expert_sems("first")
        cleared = sem("cleared")
        with nc.Block() as block:

            @block.sync
            def _(sp):
                with sp.Fori(1, NE // 2) as i:
                    for b in range(2):
                        e = 2 * i + b
                        for w, wv, used, landed in ((W1, w1_v, "gated", 0), (W3, w3_v, "upped", 1), (W2, w2_v, "downed", 2)):
                            sp.wait_ge(s_e[used], e - 1)
                            sp.dma_start(w[b], wv[bass.ds(e, 1)].rearrange("e p k f -> p (e k) f")).then_inc(expert_w[b][landed], 16)

            @block.gpsimd
            def _(pool):
                pool.memset(xg[0], 0.0).then_inc(cleared, 1)
                pool.memset(xg[1], 0.0).then_inc(cleared, 1)
                pool.wait_ge(cleared, 2)
                pool_gather(pool, s_e, 0, 0, 0)
                pool_gather(pool, s_e, 1, 1, 0)
                with pool.Fori(0, NE // 2 - 1) as i:
                    pool_gather(pool, s_e, 2 * i + 2, 0, 2 * i + 1)
                    pool_scatter(pool, s_e, 2 * i, 0)
                    pool_gather(pool, s_e, 2 * i + 3, 1, 2 * i + 2)
                    pool_scatter(pool, s_e, 2 * i + 1, 1)
                pool_scatter(pool, s_e, NE - 2, 0)
                pool_scatter(pool, s_e, NE - 1, 1)
                for b in range(2):
                    pool.wait_ge(s_e["scattered"][b], 16 * (NE // 2))

            @block.tensor
            def _(pe):
                def expert_steps(e, b, rounds, pair):
                    pe.wait_ge(expert_w[b][0], 16 * rounds)
                    pe_gate(pe, s_e, e, b)
                    if pair != "first":
                        pe_turn_hid(pe, s_e, e - 1, 1 - b)
                    pe.wait_ge(expert_w[b][1], 16 * rounds)
                    pe_up(pe, s_e, e, b)
                    if pair != "last":
                        pe_turn_x(pe, s_e, e + 1, 1 - b, rounds + b)
                    if pair != "first":
                        pe.wait_ge(expert_w[1 - b][2], 16 * (rounds - 1 + b))
                        pe_down(pe, s_e, e - 1, 1 - b)

                pe_turn_x(pe, s_e, 0, 0, 1)
                expert_steps(0, 0, 1, "first")
                with pe.Fori(0, NE // 2 - 1) as i:
                    expert_steps(2 * i + 1, 1, i + 1, "")
                    expert_steps(2 * i + 2, 0, i + 2, "")
                expert_steps(NE - 1, 1, NE // 2, "last")
                pe_turn_hid(pe, s_e, NE - 1, 1)
                pe.wait_ge(expert_w[1][2], 16 * (NE // 2))
                pe_down(pe, s_e, NE - 1, 1)

            @block.scalar
            def _(act):
                act_xT(act, s_e, 0, 0)
                act_silu(act, s_e, 0, 0)
                act_xT(act, s_e, 1, 1)
                with act.Fori(0, NE // 2 - 1) as i:
                    act_silu(act, s_e, 2 * i + 1, 1)
                    act_xT(act, s_e, 2 * i + 2, 0)
                    act_y(act, s_e, 2 * i, 0, i)
                    act_silu(act, s_e, 2 * i + 2, 0)
                    act_xT(act, s_e, 2 * i + 3, 1)
                    act_y(act, s_e, 2 * i + 1, 1, i)
                act_silu(act, s_e, NE - 1, 1)
                act_y(act, s_e, NE - 2, 0, NE // 2 - 1)
                act_y(act, s_e, NE - 1, 1, NE // 2 - 1)

            @block.vector
            def _(dve):
                dve_tokens(dve, s_e, 0, 0, 0, 0)
                dve_tokens(dve, s_e, 1, 1, 1, 0)
                dve_hid(dve, s_e, 0, 0)
                with dve.Fori(0, NE // 2 - 1) as i:
                    dve_pairs(dve, s_e, 2 * i, 0, 2 * i, i)
                    dve_hidT(dve, s_e, 2 * i, 0)
                    dve_hid(dve, s_e, 2 * i + 1, 1)
                    dve_tokens(dve, s_e, 2 * i + 2, 0, 2 * i + 2, i + 1)
                    dve_pairs(dve, s_e, 2 * i + 1, 1, 2 * i + 1, i)
                    dve_hidT(dve, s_e, 2 * i + 1, 1)
                    dve_hid(dve, s_e, 2 * i + 2, 0)
                    dve_tokens(dve, s_e, 2 * i + 3, 1, 2 * i + 3, i + 1)
                dve_pairs(dve, s_e, NE - 2, 0, NE - 2, NE // 2 - 1)
                dve_hidT(dve, s_e, NE - 2, 0)
                dve_hid(dve, s_e, NE - 1, 1)
                dve_pairs(dve, s_e, NE - 1, 1, NE - 1, NE // 2 - 1)
                dve_hidT(dve, s_e, NE - 1, 1)

        s_o = expert_sems("over")
        over_w = [sem(f"over_w{i}") for i in range(3)]
        with nc.Block() as block:

            def each_block(eng, body):
                n_over = eng.value_load(over_n[0:1, 0:1], min_val=0, max_val=OVER)
                with eng.Fori(0, OVER) as n:
                    with eng.If(n < n_over):
                        body(n)

            def column_of(eng, n):
                return eng.value_load(over_list[0:1, bass.ds(n, 1)], min_val=0, max_val=COLS - 1)

            @block.sync
            def _(sp):
                def body(n):
                    e = column_of(sp, n) % NE
                    for j, (w, wv, used) in enumerate(((W1, w1_v, "gated"), (W3, w3_v, "upped"), (W2, w2_v, "downed"))):
                        sp.wait_ge(s_o[used], n)
                        sp.dma_start(w[0], wv[bass.ds(e, 1)].rearrange("e p k f -> p (e k) f")).then_inc(over_w[j], 16)
                each_block(sp, body)

            @block.gpsimd
            def _(pool):
                def body(n):
                    pool_gather(pool, s_o, n, 0, n)
                    pool_scatter(pool, s_o, n, 0)
                    pool.wait_ge(s_o["scattered"][0], 16 * n + 16)
                each_block(pool, body)

            @block.tensor
            def _(pe):
                def body(n):
                    pe_turn_x(pe, s_o, n, 0, n + 1)
                    pe.wait_ge(over_w[0], 16 * n + 16)
                    pe_gate(pe, s_o, n, 0)
                    pe.wait_ge(over_w[1], 16 * n + 16)
                    pe_up(pe, s_o, n, 0)
                    pe_turn_hid(pe, s_o, n, 0)
                    pe.wait_ge(over_w[2], 16 * n + 16)
                    pe_down(pe, s_o, n, 0)
                each_block(pe, body)

            @block.scalar
            def _(act):
                def body(n):
                    act_xT(act, s_o, n, 0)
                    act_silu(act, s_o, n, 0)
                    act_y(act, s_o, n, 0, n)
                each_block(act, body)

            @block.vector
            def _(dve):
                def body(n):
                    col = column_of(dve, n)
                    dve_tokens(dve, s_o, n, 0, col, n)
                    dve_pairs(dve, s_o, n, 0, col, n)
                    dve_hid(dve, s_o, n, 0)
                    dve_hidT(dve, s_o, n, 0)
                each_block(dve, body)

        y_tiles = y_rows.rearrange("(m p k) d -> m p (k d)", p=P, k=2)
        yy = [at(f"yy{m}", 8 * m, [P, 2, D]) for m in range(NT)]
        y_back = [sem(f"y_back{m}") for m in range(NT)]
        combined = sem("combined")
        out_stored = sem("out_stored")
        with nc.Block() as block:

            @block.sync
            def _(sp):
                for m in range(NT):
                    sp.dma_start(yy[m].rearrange("p k d -> p (k d)"), y_tiles[m]).then_inc(y_back[m], 16)

            @block.vector
            def _(dve):
                for m in range(NT):
                    dve.wait_ge(y_back[m], 16)
                    for k in range(2):
                        if k:
                            dve.wait_ge(combined, 2 * m + 1)
                        dve.scalar_tensor_tensor(x2[:, m], yy[m][:, k], gate[k][:, m:m + 1], x2[:, m],
                                                 ALU.mult, ALU.add).then_inc(combined, 1)

            @block.scalar
            def _(act):
                for m in range(NT):
                    act.wait_ge(combined, 2 * m + 2)
                    act.dma_start(outv[m], x2[:, m]).then_inc(out_stored, 16)
                act.wait_ge(out_stored, 16 * NT)

        return dict(locals())


_INS = ['x', 'norm_mix_w', 'w_in', 'conv_w', 'q_norm_w', 'k_norm_w', 'group_norm_conv_w', 'group_norm_attn_w',
        'w_out', 'norm_ffn_w', 'w_group', 'b_group', 'w_expert', 'b_expert', 'w1', 'w3', 'w2']
_OUTS = [((1, 1024, 1024), 'float32')]


def build(nc, shapes):
    args = []
    for name in _INS:
        args.append(nc.dram_tensor(f"in_{name}_dram", shapes[name], F32, kind="ExternalInput").ap())
    for i, (shape, dtype) in enumerate(_OUTS):
        args.append(nc.dram_tensor(f"out_{i}_dram", shape, F32, kind="ExternalOutput").ap())
    return hymba_moe_layer(nc, *args)


def kernel(**inputs):
    import numpy as _np
    import concourse.bacc as _bacc
    from concourse.bass_utils import run_bass_kernel_spmd as _run

    nc = _bacc.Bacc("TRN2", target_bir_lowering=False, num_devices=1)
    arrays = {f"in_{name}_dram": _np.ascontiguousarray(inputs[name]) for name in _INS}
    build(nc, {name: inputs[name].shape for name in _INS})
    r = _run(nc, [arrays], core_ids=[0])
    return r.results[0]["out_0_dram"]
```

```python
from contextlib import ExitStack

import concourse.bass as bass
from concourse import mybir

F32 = mybir.dt.float32
F32R = mybir.dt.float32r
BF16 = mybir.dt.bfloat16
I32 = mybir.dt.int32
U32 = mybir.dt.uint32
ALU = mybir.AluOpType
ACT = mybir.ActivationFunctionType
AX = mybir.AxisListType

P = 128
BANK = 512
EPS = 1e-6
MASKED = -1e30
KIB = 1024


def hymba_moe_layer(nc, x, norm_mix_w, w_in, conv_w, q_norm_w, k_norm_w, group_norm_conv_w,
                    group_norm_attn_w, w_out, norm_ffn_w, w_group, b_group, w_expert, b_expert,
                    w1, w3, w2, out):
    S, D = x.shape[1], x.shape[2]
    KT = D // P
    NT = S // P
    CW = conv_w.shape[2]
    CB = CW // P
    TAPS = conv_w.shape[1]
    HD = q_norm_w.shape[1]
    NCH = w_in.shape[2] // CW
    HALVES = S // BANK
    NG = w_group.shape[2]
    NE = w_expert.shape[2]
    EPG = NE // NG
    F = w1.shape[3]
    FT = F // P
    PAIRS = 2 * S
    NBLK = S // P
    OVER = PAIRS // P - 1
    LOG = NG + NE
    assert D == S == KT * P and CW == 4 * P and NCH == 6 and HALVES == 2 and F == BANK

    xv = x.rearrange("a (m p) d -> (a m) p d", p=P)
    outv = out.rearrange("a (m p) d -> (a m) p d", p=P)
    w_in_v = w_in.rearrange("a (p k) n -> p (a k) n", k=KT)
    w_out_v = w_out.rearrange("a (c p) n -> p (a c) n", p=P)
    w1_v = w1.rearrange("a e (p k) f -> (a e) p k f", k=KT)
    w3_v = w3.rearrange("a e (p k) f -> (a e) p k f", k=KT)
    w2_v = w2.rearrange("a e (p k) n -> (a e) p k n", k=FT)

    xn2_rows = nc.dram_tensor("xn2_rows", (S, D), F32, kind="Internal").ap()
    y_rows = nc.dram_tensor("y_rows", (PAIRS, D), F32, kind="Internal").ap()

    with ExitStack() as ctx:
        sem = lambda name: ctx.enter_context(nc.semaphore(name))
        ps_t = ctx.enter_context(nc.psum_tensor("ps", [P, 8, BANK], F32))
        ps = ps_t[:]

        base = (nc.sbuf_base + 31) // 32 * 32
        ROOM = 205 * KIB
        ctx.enter_context(nc.sbuf_tensor("arena", [P, ROOM // 4], F32))
        names = set()

        def at(name, kib, shape, dt=F32):
            size = 4
            for n in shape[1:]:
                size *= n
            if dt == BF16:
                size //= 2
            assert name not in names and kib * KIB + size <= ROOM, name
            names.add(name)
            return nc.alloc_sbuf_tensor_at(name, shape, dt, offset=int(base + kib * KIB))[:]

        xnT_hi = at("xnT_hi", 0, [P, KT, S], F32R)
        xnT_lo = at("xnT_lo", 32, [P, KT, S], F32R)
        w_raw = [at(f"w_raw{i}", 64 + 8 * i, [P, 4, CW]) for i in range(2)]
        w_hi = at("w_hi", 80, [P, 4, CW], F32R)
        w_lo = at("w_lo", 88, [P, 4, CW], F32R)
        W1 = [at(f"W1_{i}", 48 * i, [P, KT, F]) for i in range(2)]
        W3 = [at(f"W3_{i}", 48 * i + 16, [P, KT, F]) for i in range(2)]
        W2 = [at(f"W2_{i}", 48 * i + 32, [P, FT, D]) for i in range(2)]
        NBUF = 3
        E_ = [at(f"soft{i}", 48 + 16 * i, [P, S]) for i in range(NBUF)]
        R_ = [at(f"relu{i}", 52 + 16 * i, [P, S]) for i in range(NBUF)]
        G_ = [at(f"suffix{i}", 56 + 16 * i, [P, S]) for i in range(NBUF)]
        AT_ = [at(f"probsT{i}", 60 + 16 * i, [P, NT, P]) for i in range(NBUF)]
        w_out_sb = at("w_out_sb", 48, [P, 2 * CB, D])
        yT = [at(f"yT{i}", 80 + 4 * i, [P, 2 * CB, P]) for i in range(2)]
        xn2 = [at(f"xn2_{i}", 88 + 4 * i, [P, D]) for i in range(2)]
        xn2T = [at(f"xn2T_{i}", 32 + 4 * i, [P, KT, P]) for i in range(2)]
        g2b = at("g2b", 40, [P, D])
        sq2 = at("sq2", 44, [P, D])

        small = [96 * KIB]

        def keep(name, shape, dt=F32):
            size = 4
            for n in shape[1:]:
                size *= n
            kib = small[0] / KIB
            small[0] += (size + 31) // 32 * 32
            assert small[0] <= 103.5 * KIB
            return at(name, kib, shape, dt)

        ident = keep("ident", [P, P])
        same_head = keep("same_head", [P, P])
        identr = keep("identr", [P, P], F32R)
        maskr = keep("maskr", [P, P], F32R)
        eps = keep("eps", [P, 1])
        ss = keep("ss", [P, 2])
        rt = keep("rt", [P, 2])
        rr = keep("rr", [P, 2])
        gains = keep("gains", [P, 12])
        gain_attn = keep("gain_attn", [P, CB])
        taps = keep("taps", [P, TAPS, CB])
        router_w = keep("router_w", [P, KT, LOG])
        router_b = keep("router_b", [P, LOG])

        u = at("u", 103.5, [P, CB, S + TAPS - 1])
        v = at("v", 103.5, [P, NT, CW])
        big = at("big", 120, [P, 12, S])
        T0 = 168
        xt = [at(f"xt{i}", T0 + 4 * i, [P, D]) for i in range(2)]
        xn = [at(f"xn{i}", T0 + 8 + 4 * i, [P, D]) for i in range(2)]
        g1b = at("g1b", T0 + 16, [P, D])
        sq1 = at("sq1", T0 + 20, [P, D])
        conv = at("conv", T0 + 24, [P, S])
        nsq = [at(f"nsq{i}", 80 + 4 * i, [P, S]) for i in range(2)]
        nrt = [at(f"nrt{i}", 88 + 4 * i, [P, S]) for i in range(2)]
        q_hi, q_lo, k_hi, k_lo = ([at(f"{n}{i}", kib + 4 * j, [P, S], F32R) for i, kib in enumerate((T0, 32))]
                                  for j, n in enumerate(("q_hi", "q_lo", "k_hi", "k_lo")))
        v_pair = [at(f"v_pair{i}", T0 + 16 + 4 * i, [P, NT, P]) for i in range(2)]
        x2 = at("x2", T0, [P, NT, D])
        logits = keep("logits", [P, NT, LOG])

        psf = ps.rearrange("p a b -> p (a b)")

        may_start = sem("may_start")

        def start_step(pool):
            pool.sem_inc(may_start, 1)

        consts_in = sem("consts_in")
        consts_made = sem("consts_made")
        x_landed = [sem(f"x_landed{i}") for i in range(2)]
        x_squared = sem("x_squared")
        x_rooted = sem("x_rooted")
        x_inverse = sem("x_inverse")
        x_scaled = sem("x_scaled")
        x_turned = sem("x_turned")
        x_hi_made = sem("x_hi_made")
        w_landed = [sem(f"w_landed{i}") for i in range(2)]
        w_hi_made = sem("w_hi_made")
        w_lo_made = sem("w_lo_made")
        w_used = sem("w_used")
        banks_filled = sem("banks_filled")
        banks_read = sem("banks_read")
        u_made = sem("u_made")
        conv_step = sem("conv_step")
        router_in = sem("router_in")

        with nc.Block(no_gpsimd_drain=True) as block:

            @block.sync
            def _(sp):
                for i in range(2):
                    sp.dma_start(xt[i], xv[i]).then_inc(x_landed[i], 16)
                sp.dma_start(g1b, norm_mix_w.partition_broadcast(P)[:, 0, :]).then_inc(consts_in, 16)
                for h in range(2):
                    rows = slice(h * HD, (h + 1) * HD)
                    sp.dma_start(gains[rows, 4:5], q_norm_w.rearrange("a d -> d a")).then_inc(consts_in, 16)
                    sp.dma_start(gains[rows, 8:9], k_norm_w.rearrange("a d -> d a")).then_inc(consts_in, 16)
                with nc.allow_non_contiguous_dma(reason="small columns"):
                    sp.dma_start(gains[:, 0:4], group_norm_conv_w.rearrange("a (b g) d -> (g d) (a b)", g=2)).then_inc(consts_in, 16)
                    sp.dma_start(gain_attn, group_norm_attn_w.rearrange("a (b g) d -> (g d) (a b)", g=2)).then_inc(consts_in, 16)
                    for j in range(TAPS):
                        sp.dma_start(taps[:, j, :], conv_w[0, j].rearrange("(b p) -> p b", p=P)).then_inc(consts_in, 16)
                for hf in range(2):
                    sp.dma_start(w_raw[hf], w_in_v[:, 4 * hf:4 * hf + 4, 0:CW]).then_inc(w_landed[hf], 16)
                with nc.allow_non_contiguous_dma(reason="small columns"):
                    sp.dma_start(router_w[:, :, 0:NG], w_group.rearrange("a (p k) g -> p (a k) g", k=KT)).then_inc(router_in, 16)
                    sp.dma_start(router_w[:, :, NG:], w_expert.rearrange("a (p k) g -> p (a k) g", k=KT)).then_inc(router_in, 16)
                with sp.Fori(1, NT // 2) as i:
                    for b in range(2):
                        sp.wait_ge(x_scaled, 2 * i + b - 1)
                        sp.dma_start(xt[b], xv[bass.ds(2 * i + b, 1)].rearrange("m p d -> p (m d)")).then_inc(x_landed[b], 16)
                with sp.Fori(1, NCH) as c:
                    for hf in range(2):
                        sp.wait_ge(w_lo_made, 8 * c + 4 * hf - 4)
                        sp.dma_start(w_raw[hf], w_in_v[:, 4 * hf:4 * hf + 4, bass.ds(c * CW, CW)]).then_inc(w_landed[hf], 16)
                sp.dma_start(router_b[:, 0:NG], b_group.partition_broadcast(P)[:, 0, :]).then_inc(router_in, 16)
                sp.dma_start(router_b[:, NG:], b_expert.partition_broadcast(P)[:, 0, :]).then_inc(router_in, 16)
                sp.wait_ge(router_in, 16 * 4)

            @block.gpsimd
            def _(pool):
                pool.memset(ident, 0.0).then_inc(consts_made, 1)
                pool.memset(maskr.bitcast(F32), 0.0).then_inc(consts_made, 1)
                pool.memset(same_head, 0.0).then_inc(consts_made, 1)
                pool.memset(eps, EPS).then_inc(consts_made, 1)
                pool.memset(u[:, :, 0:TAPS - 1], 0.0).then_inc(consts_made, 1)
                pool.wait_ge(consts_made, 5)
                pool.affine_select(out=ident, in_=ident, compare_op=ALU.not_equal, fill=1.0, base=0,
                                   pattern=[[-1, P]], channel_multiplier=1).then_inc(consts_made, 1)
                pool.wait_ge(consts_made, 6)
                pool.memset(same_head[0:HD, 0:HD], 1.0).then_inc(consts_made, 1)
                pool.wait_ge(consts_made, 7)
                pool.memset(same_head[HD:P, HD:P], 1.0).then_inc(consts_made, 1)
                pool.wait_ge(consts_made, 8)
                pool.tensor_copy(identr, ident).then_inc(consts_made, 1)
                pool.affine_select(out=maskr, in_=maskr.bitcast(F32), compare_op=ALU.is_gt, fill=MASKED, base=0,
                                   pattern=[[-1, P]], channel_multiplier=1).then_inc(consts_made, 1)

            @block.scalar
            def _(act):
                act.wait_ge(consts_made, 10)
                with act.Fori(0, NT // 2) as i:
                    for b in range(2):
                        act.wait_ge(x_landed[b], 16 * i + 16)
                        act.activation(sq1, xt[b], ACT.Square, accum_out=ss[:, b:b + 1]).then_inc(x_squared, 1)
                        act.wait_ge(x_squared, 2 * i + b + 1)
                        act.activation(rt[:, b:b + 1], ss[:, b:b + 1], ACT.Sqrt, bias=eps, scale=1.0 / D).then_inc(x_rooted, 1)
                    for b in range(2):
                        act.wait_ge(x_turned, 2 * i + b + 1)
                        act.activation(xnT_hi[:, :, bass.ds((2 * i + b) * P, P)],
                                       psf[:, b * D:(b + 1) * D].rearrange("p (k t) -> p k t", k=KT),
                                       ACT.Copy).then_inc(x_hi_made, 1)

                def split(c, k):
                    if k % 4 == 0:
                        act.wait_ge(w_landed[k // 4], 16 * (c + 1))
                    if k >= 4:
                        act.wait_ge(w_used, 7 * c + k - 3)
                    elif c and k < 3:
                        act.wait_ge(w_used, 7 * (c - 1) + k + 5)
                    elif c:
                        act.wait_ge(banks_filled, 8 * c)
                    act.activation(w_hi[:, k % 4], w_raw[k // 4][:, k % 4], ACT.Copy).then_inc(w_hi_made, 1)

                def empty(c):
                    for b in range(8):
                        act.wait_ge(banks_filled, 8 * c + b + 1)
                        if c == 5:
                            dst = v[:, b, :]
                            if b == 0:
                                act.wait_ge(conv_step, 4 * CB)
                        elif c == 1:
                            h = b % 2
                            dst = u[:, b // 2, TAPS - 1 + h * BANK:TAPS - 1 + (h + 1) * BANK]
                        else:
                            row = {0: 0, 3: 4, 4: 8}[c] + b // 2
                            dst = big[:, row, (b % 2) * BANK:(b % 2 + 1) * BANK]
                        act.activation(dst, ps[:, b], ACT.Copy).then_inc(banks_read, 1)

                for c in range(NCH):
                    for k in range(8):
                        if k == 3 and c and c - 1 != 2:
                            empty(c - 1)
                        split(c, k)
                empty(NCH - 1)

            @block.vector
            def _(dve):
                dve.wait_ge(consts_in, 16 * 10)
                with dve.Fori(0, NT // 2) as i:
                    for b in range(2):
                        dve.wait_ge(x_rooted, 2 * i + b + 1)
                        dve.reciprocal(rr[:, b:b + 1], rt[:, b:b + 1]).then_inc(x_inverse, 1)
                        dve.wait_ge(x_inverse, 2 * i + b + 1)
                        dve.wait_ge(x_turned, 2 * i)
                        dve.scalar_tensor_tensor(xn[b], xt[b], rr[:, b:b + 1], g1b, ALU.mult, ALU.mult).then_inc(x_scaled, 1)
                    for b in range(2):
                        dve.wait_ge(x_hi_made, 2 * i + b + 1)
                        cols = bass.ds((2 * i + b) * P, P)
                        dve.tensor_tensor(xnT_lo[:, :, cols], psf[:, b * D:(b + 1) * D].rearrange("p (k t) -> p k t", k=KT),
                                          xnT_hi[:, :, cols].bitcast(F32), ALU.subtract).then_inc(banks_read, 1)

                def convolve(j):
                    n = 4 * j
                    for tap in range(TAPS):
                        src = u[:, j, tap:tap + S]
                        w = taps[:, tap, j:j + 1]
                        if tap == 0:
                            if j:
                                dve.wait_ge(conv_step, n)
                            dve.tensor_scalar(conv, src, w, None, ALU.mult).then_inc(conv_step, 1)
                        else:
                            dve.wait_ge(conv_step, n + tap)
                            dve.scalar_tensor_tensor(conv, src, w, conv, ALU.mult, ALU.add).then_inc(conv_step, 1)
                    dve.wait_ge(conv_step, n + 3)
                    dve.tensor_tensor(big[:, j], big[:, j], conv, ALU.mult).then_inc(conv_step, 1)

                for c in range(NCH):
                    for k in range(8):
                        if k == 3 and c - 1 == 2:
                            for b in range(8):
                                dve.wait_ge(banks_filled, 8 * (c - 1) + b + 1)
                                dve.wait_ge(banks_read, 8 + 16)
                                h = b % 2
                                dst = u[:, b // 2, TAPS - 1 + h * BANK:TAPS - 1 + (h + 1) * BANK]
                                dve.tensor_tensor(dst, ps[:, b], dst, ALU.mult).then_inc(banks_read, 1)
                            dve.wait_ge(banks_read, 8 + 24)
                        dve.wait_ge(w_hi_made, 8 * c + k + 1)
                        dve.tensor_tensor(w_lo[:, k % 4], w_raw[k // 4][:, k % 4], w_hi[:, k % 4].bitcast(F32),
                                          ALU.subtract).then_inc(w_lo_made, 1)
                        if c == 3 and k >= 4:
                            convolve(k - 4)

            @block.tensor
            def _(pe):
                pe.wait_ge(consts_made, 10)
                with pe.Fori(0, NT // 2) as i:
                    for b in range(2):
                        pe.wait_ge(x_scaled, 2 * i + b + 1)
                        pe.wait_ge(banks_read, 2 * i)
                        for k in range(KT):
                            t = pe.transpose(psf[:, b * D + k * P:b * D + (k + 1) * P], xn[b][:, k:D:KT], ident)
                        t.then_inc(x_turned, 1)
                pe.wait_ge(banks_read, NT)
                THREE = [("hi", "hi"), ("hi", "lo"), ("lo", "hi")]
                with pe.Fori(0, NCH - 1) as c:
                    for k in range(KT):
                        pe.wait_ge(w_lo_made, 8 * c + k + 1)
                        for b in range(8):
                            if k == 0:
                                pe.wait_ge(banks_read, 8 * c + b + 1)
                            for j, (a, z) in enumerate(THREE):
                                w = (w_hi if a == "hi" else w_lo)[:, k % 4, (b // 2) * P:(b // 2 + 1) * P]
                                r = (xnT_hi if z == "hi" else xnT_lo)[:, k, (b % 2) * BANK:(b % 2 + 1) * BANK]
                                mm = pe.matmul(ps[:, b], w, r, start=(k == 0 and j == 0), stop=(k == KT - 1 and j == 2))
                            if k == KT - 1:
                                mm.then_inc(banks_filled, 1)
                        if k < KT - 1:
                            mm.then_inc(w_used, 1)
                c = NCH - 1
                for k in range(KT):
                    pe.wait_ge(w_lo_made, 8 * c + k + 1)
                    for b in range(8):
                        if k == 0:
                            pe.wait_ge(banks_read, 8 * c + b + 1)
                        for j, (a, z) in enumerate(THREE):
                            w = (w_hi if a == "hi" else w_lo)[:, k % 4]
                            r = (xnT_hi if z == "hi" else xnT_lo)[:, k, b * P:(b + 1) * P]
                            mm = pe.matmul(ps[:, b], r, w, start=(k == 0 and j == 0), stop=(k == KT - 1 and j == 2))
                        if k == KT - 1:
                            mm.then_inc(banks_filled, 1)
                    if k < KT - 1:
                        mm.then_inc(w_used, 1)

        def norm_sems(tag):
            return {n: sem(f"{tag}_{n}") for n in ("squared", "summed", "logged", "inverted", "scaled")}

        def norm_scalar(act, s, first, last, row):
            with act.Fori(first, last) as i:
                for b in range(2):
                    act.wait_ge(s["summed"], 4 * i)
                    act.activation(nsq[b], big[:, bass.ds(2 * i + b + row, 1)].rearrange("p a t -> p (a t)"),
                                   ACT.Square).then_inc(s["squared"], 1)
                for b in range(2):
                    act.wait_ge(s["summed"], 4 * i + 2 * b + 2)
                    act.wait_ge(s["scaled"], 2 * i)
                    act.activation(nrt[b], psf[:, b * S:(b + 1) * S], ACT.Ln, bias=eps, scale=1.0 / HD).then_inc(s["logged"], 1)
                for b in range(2):
                    act.wait_ge(s["logged"], 2 * i + b + 1)
                    act.activation(nrt[b], nrt[b], ACT.Exp, scale=-0.5).then_inc(s["inverted"], 1)

        def norm_tensor(pe, s, n):
            with pe.Fori(0, n) as i:
                for b in range(2):
                    pe.wait_ge(s["squared"], 2 * i + b + 1)
                    pe.wait_ge(s["logged"], 2 * i)
                    for h in range(2):
                        pe.matmul(ps[:, 2 * b + h], same_head, nsq[b][:, h * BANK:(h + 1) * BANK],
                                  start=True, stop=True).then_inc(s["summed"], 1)

        def norm_vector(dve, s, first, last, row, gain, g0):
            with dve.Fori(first, last) as i:
                for b in range(2):
                    blk = big[:, bass.ds(2 * i + b + row, 1)].rearrange("p a t -> p (a t)")
                    dve.wait_ge(s["inverted"], 2 * i + b + 1)
                    dve.scalar_tensor_tensor(blk, blk, gain[:, bass.ds(2 * i + b + g0, 1)], nrt[b],
                                             ALU.mult, ALU.mult).then_inc(s["scaled"], 1)

        s_n1 = norm_sems("norm1")
        gains_made = sem("gains_made")
        staged = sem("staged")
        scored = sem("scored")
        valued = sem("valued")
        UNITS_OF_PAIR = 2 * NT
        UNITS = 2 * UNITS_OF_PAIR

        def stage(pool, r):
            for i in range(2):
                q, k = big[:, 2 * r + i + CB], big[:, 2 * r + i + 2 * CB]
                if r:
                    pool.wait_ge(scored, UNITS * r - (1 - i) * UNITS_OF_PAIR)
                pool.tensor_copy(q_hi[i], q).then_inc(staged, 1)
                pool.tensor_copy(k_hi[i], k).then_inc(staged, 1)
                pool.wait_ge(staged, 10 * r + 5 * i + 2)
                pool.tensor_tensor(q_lo[i], q, q_hi[i].bitcast(F32), ALU.subtract).then_inc(staged, 1)
                pool.tensor_tensor(k_lo[i], k, k_hi[i].bitcast(F32), ALU.subtract).then_inc(staged, 1)
                if r:
                    pool.wait_ge(valued, UNITS * r - (1 - i) * UNITS_OF_PAIR)
                pool.tensor_copy(v_pair[i], v[:, :, (2 * r + i) * P:(2 * r + i + 1) * P]).then_inc(staged, 1)

        with nc.Block(no_gpsimd_drain=True) as block:

            @block.gpsimd
            def _(pool):
                pool.wait_ge(s_n1["scaled"], 2 * CB)
                stage(pool, 0)

            @block.scalar
            def _(act):
                norm_scalar(act, s_n1, 0, 4, CB)
                norm_scalar(act, s_n1, 4, 6, -2 * CB)

            @block.tensor
            def _(pe):
                norm_tensor(pe, s_n1, 6)

            @block.vector
            def _(dve):
                dve.tensor_scalar(gains[:, 4:5], gains[:, 4:5], float(HD) ** -0.5, None, ALU.mult).then_inc(gains_made, 1)
                dve.wait_ge(gains_made, 1)
                for j in range(1, CB):
                    dve.tensor_copy(gains[:, 4 + j:5 + j], gains[:, 4:5]).then_inc(gains_made, 1)
                    dve.tensor_copy(gains[:, 8 + j:9 + j], gains[:, 8:9]).then_inc(gains_made, 1)
                dve.wait_ge(gains_made, 2 * CB - 1)
                norm_vector(dve, s_n1, 0, 4, CB, gains, CB)
                norm_vector(dve, s_n1, 4, 6, -2 * CB, gains, -2 * CB)

        GROUP = 8
        absolute = sem("absolute")
        small_exp = sem("small_exp")
        small_ln = sem("small_ln")
        relued = sem("relued")
        summed = sem("summed")
        logged = sem("logged")
        weighed = sem("weighed")
        turned = sem("turned")
        turned_read = sem("turned_read")
        out_read = sem("out_read")
        w_in_e = {}
        L = lambda n: (n % UNITS_OF_PAIR // 2 + 1) * P
        TH = sum((L(n) + BANK - 1) // BANK for n in range(UNITS))
        th_before = [sum((L(m) + BANK - 1) // BANK for m in range(n)) for n in range(UNITS + 1)]
        ZBUF = 2
        TBANKS = (4, 5, 6)
        assert TH % len(TBANKS) == 0 and UNITS % ZBUF == 0
        ZB = lambda n: psf[:, (n % ZBUF) * S:(n % ZBUF) * S + L(n)]
        TB = lambda g: ps[:, TBANKS[g % len(TBANKS)]]
        expert_w = [[sem(f"expert_w{m}_{i}") for m in (1, 3, 2)] for i in range(2)]

        with nc.Block(no_gpsimd_drain=True) as block:

            @block.sync
            def _(sp):
                sp.dma_start(W1[0], w1_v[0]).then_inc(expert_w[0][0], 16)
                sp.dma_start(W3[0], w3_v[0]).then_inc(expert_w[0][1], 16)

            @block.gpsimd
            def _(pool):
                stage(pool, 1)

            @block.tensor
            def _(pe):
                def scores(p, n):
                    i, t, h = n // UNITS_OF_PAIR, n % UNITS_OF_PAIR // 2, n % 2
                    rows = slice(h * HD, (h + 1) * HD)
                    if n % UNITS_OF_PAIR == 0:
                        pe.wait_ge(staged, 10 * p + 5 * i + 4)
                    if n >= ZBUF:
                        pe.wait_ge(logged, UNITS * p + n - ZBUF + 1)
                    else:
                        pe.wait_ge(logged, UNITS * p)
                    z = ZB(n)
                    for c0 in range(0, L(n), BANK):
                        c1 = min(c0 + BANK, L(n))
                        last = c1 == L(n)
                        cols = slice(t * P, (t + 1) * P)
                        pe.matmul(z[:, c0:c1], q_hi[i][rows, cols], k_hi[i][rows, c0:c1], start=True, stop=False)
                        pe.matmul(z[:, c0:c1], q_hi[i][rows, cols], k_lo[i][rows, c0:c1], start=False, stop=False)
                        mm = pe.matmul(z[:, c0:c1], q_lo[i][rows, cols], k_hi[i][rows, c0:c1], start=False, stop=not last)
                    mm = pe.matmul(z[:, L(n) - P:L(n)], identr, maskr, start=False, stop=True)
                    mm.then_inc(scored, 1)

                def turn(p, n, half):
                    g = th_before[n] + half
                    if half == 0:
                        pe.wait_ge(weighed, UNITS * p + n + 1)
                    if g >= len(TBANKS):
                        pe.wait_ge(turned_read, TH * p + g - len(TBANKS) + 1)
                    else:
                        pe.wait_ge(turned_read, TH * p)
                    for j in range(4 * half, min(4 * half + 4, L(n) // P)):
                        mm = pe.transpose(TB(g)[:, (j % 4) * P:(j % 4 + 1) * P], G_[n % NBUF][:, j * P:(j + 1) * P], ident)
                    mm.then_inc(turned, 1)

                def values(p, n):
                    i, t, h = n // UNITS_OF_PAIR, n % UNITS_OF_PAIR // 2, n % 2
                    if n % UNITS_OF_PAIR == 0:
                        pe.wait_ge(staged, 10 * p + 5 * i + 5)
                    pe.wait_ge(turned_read, TH * p + th_before[n + 1])
                    if n % GROUP == 0:
                        pe.wait_ge(out_read, UNITS // GROUP * p + n // GROUP)
                    for j in range(t + 1):
                        mm = pe.matmul(ps[h * HD:(h + 1) * HD, 7, (t % 4) * P:(t % 4 + 1) * P],
                                       v_pair[i][:, j, h * HD:(h + 1) * HD], AT_[n % NBUF][:, j, :],
                                       start=(j == 0), stop=(j == t))
                    mm.then_inc(valued, 1)

                with pe.Fori(0, CB // 2) as p:
                    for n in range(-1, UNITS + 2):
                        if n + 1 < UNITS:
                            scores(p, n + 1)
                        if n >= 2:
                            values(p, n - 2)
                        if 1 <= n <= UNITS:
                            for half in range(th_before[n] - th_before[n - 1]):
                                turn(p, n - 1, half)

            @block.scalar
            def _(act):
                def step(p, n):
                    if 1 <= n:
                        act.wait_ge(logged, UNITS * p + n)
                        g = G_[(n - 1) % NBUF][:, :L(n - 1)]
                        act.activation(g, g, ACT.Exp).then_inc(weighed, 1)
                    if n + 1 < UNITS:
                        m = n + 1
                        e = E_[m % NBUF][:, :L(m)]
                        act.wait_ge(scored, UNITS * p + m + 1)
                        if m >= NBUF:
                            act.wait_ge(logged, UNITS * p + m - NBUF + 1)
                        else:
                            act.wait_ge(logged, UNITS * p)
                        act.activation(e, ZB(m), ACT.Abs).then_inc(absolute, 1)
                        act.wait_ge(absolute, UNITS * p + m + 1)
                        act.activation(e, e, ACT.Exp, scale=-1.0).then_inc(small_exp, 1)
                        act.wait_ge(small_exp, UNITS * p + m + 1)
                        act.activation(e, e, ACT.Ln, bias=1.0).then_inc(small_ln, 1)

                with act.Fori(0, CB // 2) as p:
                    for n in range(-1, UNITS + 1):
                        step(p, n)
                        if n % GROUP == 2 and n > GROUP or n == UNITS:
                            g = (n - 2) // GROUP - 1 if n < UNITS else UNITS // GROUP - 1
                            act.wait_ge(valued, UNITS * p + GROUP * (g + 1))
                            act.activation(big[:, bass.ds(2 * p + g // 2 + CB, 1), g % 2 * BANK:(g % 2 + 1) * BANK].rearrange("p a t -> p (a t)"),
                                           ps[:, 7], ACT.Copy).then_inc(out_read, 1)

            @block.vector
            def _(dve):
                def step(p, n):
                    if 0 <= n < UNITS:
                        dve.wait_ge(small_ln, UNITS * p + n + 1)
                        dve.wait_ge(relued, UNITS * p + n + 1)
                        if n >= NBUF:
                            dve.wait_ge(turned, TH * p + th_before[n - NBUF + 1])
                        else:
                            dve.wait_ge(turned, TH * p)
                        g, e, r = (b[n % NBUF][:, L(n) - 1::-1] for b in (G_, E_, R_))
                        dve.tensor_tensor_scan(g, e, r, 0.0, ALU.add, ALU.add).then_inc(summed, 1)
                        dve.wait_ge(summed, UNITS * p + n + 1)
                        g = G_[n % NBUF][:, :L(n)]
                        dve.tensor_tensor(g, ZB(n), g, ALU.subtract).then_inc(logged, 1)
                    if 1 <= n:
                        m = n - 1
                        for hf in range(th_before[m + 1] - th_before[m]):
                            g = th_before[m] + hf
                            dve.wait_ge(turned, TH * p + g + 1)
                            if hf == 0:
                                dve.wait_ge(valued, UNITS * p + max(m - NBUF + 1, 0))
                            k0, k1 = 4 * hf, min(4 * hf + 4, L(m) // P)
                            dve.tensor_copy(AT_[m % NBUF][:, k0:k1, :],
                                            TB(g)[:, 0:(k1 - k0) * P].rearrange("p (k t) -> p k t", t=P)).then_inc(turned_read, 1)
                    if n + 1 < UNITS:
                        m = n + 1
                        dve.wait_ge(absolute, UNITS * p + m + 1)
                        dve.tensor_scalar(R_[m % NBUF][:, :L(m)], ZB(m), 0.0, None, ALU.max).then_inc(relued, 1)

                with dve.Fori(0, CB // 2) as p:
                    for n in range(-1, UNITS + 1):
                        step(p, n)

        s_n2 = norm_sems("norm2")
        w_out_in = sem("w_out_in")
        with nc.Block(no_gpsimd_drain=True) as block:

            @block.sync
            def _(sp):
                sp.dma_start(w_out_sb, w_out_v).then_inc(w_out_in, 16)

            @block.scalar
            def _(act):
                norm_scalar(act, s_n2, 0, CB // 2, CB)

            @block.tensor
            def _(pe):
                norm_tensor(pe, s_n2, CB // 2)

            @block.vector
            def _(dve):
                norm_vector(dve, s_n2, 0, CB // 2, CB, gain_attn, 0)

        x_in = sem("x_in")
        g2_in = sem("g2_in")
        y_staged = sem("y_staged")
        mixed = sem("mixed")
        x2_made = sem("x2_made")
        x2_squared = sem("x2_squared")
        x2_rooted = sem("x2_rooted")
        x2_inverse = sem("x2_inverse")
        xn2_made = sem("xn2_made")
        xn2_turned = sem("xn2_turned")
        xn2T_made = sem("xn2T_made")
        logits_summed = sem("logits_summed")
        logits_made = sem("logits_made")
        xn2_stored = [sem(f"xn2_stored{i}") for i in range(2)]
        xn2_rows_v = xn2_rows.rearrange("(m p) d -> m p d", p=P)
        x_all = x.rearrange("a (m p) d -> p (a m) d", p=P)
        one = lambda a: a.rearrange("p a d -> p (a d)")

        with nc.Block(no_gpsimd_drain=True) as block:

            @block.sync
            def _(sp):
                sp.dma_start(x2, x_all).then_inc(x_in, 16)
                sp.dma_start(g2b, norm_ffn_w.partition_broadcast(P)[:, 0, :]).then_inc(g2_in, 16)
                with sp.Fori(0, NT // 2) as i:
                    for b in range(2):
                        sp.wait_ge(xn2_made, 2 * i + b + 1)
                        sp.dma_start(xn2_rows_v[bass.ds(2 * i + b, 1)].rearrange("m p d -> p (m d)"), xn2[b]).then_inc(xn2_stored[b], 16)
                for b in range(2):
                    sp.wait_ge(xn2_stored[b], 16 * (NT // 2))

            @block.gpsimd
            def _(pool):
                with pool.Fori(0, NT // 2) as i:
                    for b in range(2):
                        pool.wait_ge(mixed, 4 * i)
                        pool.tensor_copy(yT[b], big[:, 0:2 * CB, bass.ds((2 * i + b) * P, P)]).then_inc(y_staged, 1)

            @block.tensor
            def _(pe):
                pe.wait_ge(w_out_in, 16)

                def multiply(m, b):
                    pe.wait_ge(y_staged, m + 1)
                    for h in range(2):
                        if not (isinstance(m, int) and m < 2):
                            pe.wait_ge(x2_made, 2 * m + h - 3)
                        for c in range(2 * CB):
                            mm = pe.matmul(ps[:, 2 * b + h], yT[b][:, c], w_out_sb[:, c, h * BANK:(h + 1) * BANK],
                                           start=(c == 0), stop=(c == 2 * CB - 1))
                        mm.then_inc(mixed, 1)

                def route(m, b):
                    pe.wait_ge(xn2_made, m + 1)
                    pe.wait_ge(xn2T_made, m)
                    for k in range(KT):
                        mm = pe.transpose(psf[:, 4 * BANK + k * P:4 * BANK + (k + 1) * P], xn2[b][:, k:D:KT], ident)
                    mm.then_inc(xn2_turned, 1)
                    pe.wait_ge(xn2T_made, m + 1)
                    if not (isinstance(m, int) and m < 2):
                        pe.wait_ge(logits_made, m - 1)
                    for k in range(KT):
                        mm = pe.matmul(ps[:, 6 + b, 0:LOG], xn2T[b][:, k], router_w[:, k], start=(k == 0), stop=(k == KT - 1))
                    mm.then_inc(logits_summed, 1)

                multiply(0, 0)
                multiply(1, 1)
                route(0, 0)
                with pe.Fori(1, NT // 2) as i:
                    multiply(2 * i, 0)
                    route(2 * i - 1, 1)
                    multiply(2 * i + 1, 1)
                    route(2 * i, 0)
                route(NT - 1, 1)

            @block.scalar
            def _(act):
                def turned_out(m, b):
                    act.wait_ge(xn2_turned, m + 1)
                    if not (isinstance(m, int) and m < 2):
                        act.wait_ge(logits_summed, m - 1)
                    act.activation(xn2T[b].rearrange("p k t -> p (k t)"), psf[:, 4 * BANK:6 * BANK], ACT.Copy).then_inc(xn2T_made, 1)

                def square(m, b):
                    act.wait_ge(x2_made, 2 * m + 2)
                    act.activation(sq2, one(x2[:, bass.ds(m, 1)]), ACT.Square, accum_out=ss[:, b:b + 1]).then_inc(x2_squared, 1)
                    act.wait_ge(x2_squared, m + 1)
                    act.activation(rt[:, b:b + 1], ss[:, b:b + 1], ACT.Sqrt, bias=eps, scale=1.0 / D).then_inc(x2_rooted, 1)

                square(0, 0)
                square(1, 1)
                turned_out(0, 0)
                with act.Fori(1, NT // 2) as i:
                    square(2 * i, 0)
                    turned_out(2 * i - 1, 1)
                    square(2 * i + 1, 1)
                    turned_out(2 * i, 0)
                turned_out(NT - 1, 1)

            @block.vector
            def _(dve):
                dve.wait_ge(x_in, 16)
                dve.wait_ge(g2_in, 16)
                dve.wait_ge(router_in, 64)

                def add(m, b):
                    for h in range(2):
                        dve.wait_ge(mixed, 2 * m + h + 1)
                        half = one(x2[:, bass.ds(m, 1), h * BANK:(h + 1) * BANK])
                        dve.tensor_tensor(half, ps[:, 2 * b + h], half, ALU.add).then_inc(x2_made, 1)
                    dve.wait_ge(x2_rooted, m + 1)
                    dve.reciprocal(rr[:, b:b + 1], rt[:, b:b + 1]).then_inc(x2_inverse, 1)
                    dve.wait_ge(x2_inverse, m + 1)
                    if not (isinstance(m, int) and m < 2):
                        dve.wait_ge(xn2_turned, m - 1)
                        dve.wait_ge(xn2_stored[b], (m // 2) * 16 if isinstance(m, int) else (m - b) * 8)
                    dve.scalar_tensor_tensor(xn2[b], one(x2[:, bass.ds(m, 1)]), rr[:, b:b + 1], g2b, ALU.mult, ALU.mult).then_inc(xn2_made, 1)

                def bias(m, b):
                    dve.wait_ge(logits_summed, m + 1)
                    dve.tensor_tensor(one(logits[:, bass.ds(m, 1)]), ps[:, 6 + b, 0:LOG], router_b, ALU.add).then_inc(logits_made, 1)

                add(0, 0)
                add(1, 1)
                bias(0, 0)
                with dve.Fori(1, NT // 2) as i:
                    add(2 * i, 0)
                    bias(2 * i - 1, 1)
                    add(2 * i + 1, 1)
                    bias(2 * i, 0)
                bias(NT - 1, 1)

        room = [int(103.5 * KIB)]

        def place(name, shape, dt=F32):
            size = 4
            for n in shape[1:]:
                size *= n
            kib = room[0] / KIB
            room[0] += (size + 31) // 32 * 32
            assert room[0] <= T0 * KIB
            return at(name, kib, shape, dt)

        COLS = NBLK * NE
        iota = place("iota", [P, COLS])
        iota_p1 = place("iota_p1", [P, 1])
        pair_code = [place(f"pair_code{k}", [P, NT]) for k in range(2)]
        past = place("past", [P, NBLK - 1, NE])
        before = place("before", [P, P], BF16)
        ones = place("ones", [P, P], BF16)
        d4 = place("d4", [P, NT, NG])
        e4 = place("e4", [P, NT, NG])
        c4 = place("c4", [P, NT, NG])
        of_group = place("of_group", [P, NT, NG])
        picked = place("picked", [P, NT, NG, EPG])
        sel = [place(f"sel{k}", [P, NT, EPG]) for k in range(2)]
        c8 = place("c8", [P, NT, EPG])
        of_choice = place("of_choice", [P, NT, EPG])
        top = [place(f"top{k}", [P, NT]) for k in range(3)]
        which = [place(f"which{k}", [P, NT]) for k in range(3)]
        e_diff = place("e_diff", [P, NT])
        p_group = place("p_group", [P, NT])
        gate = [keep(f"gate{k}", [P, NT]) for k in range(2)]
        expert = [place(f"expert{k}", [P, NT]) for k in range(2)]
        of_expert = [place(f"of_expert{k}", [P, NT, NE]) for k in range(2)]
        chosen = place("chosen", [P, NT, NE], BF16)
        ranked = place("ranked", [P, NT, NE])
        rank = [place(f"rank{k}", [P, NT]) for k in range(2)]
        rank_i = place("rank_i", [P, NT], I32)
        part_i = place("part_i", [P, NT], I32)
        column = [place(f"column{k}", [P, NT]) for k in range(2)]
        slot = [place(f"slot{k}", [P, NT]) for k in range(2)]
        NOH = 4
        of_slot = [place(f"of_slot{i}", [P, P], F32R) for i in range(NOH)]
        of_column = [place(f"of_column{i}", [P, COLS], F32R) for i in range(NOH)]
        unused = place("unused", [P, COLS])
        pair_f = place("pair_f", [P, COLS])
        over = place("over", [P, NBLK - 1, NE])
        over_at = place("over_at", [P, (NBLK - 1) * NE])
        over_sel = place("over_sel", [P, (NBLK - 1) * NE])
        over_col = place("over_col", [P, 1])
        slot_pair = keep("slot_pair", [P, COLS], I32)
        slot_token = keep("slot_token", [P, COLS], I32)
        over_list = keep("over_list", [1, OVER + 1], I32)
        over_n = keep("over_n", [1, 1], I32)

        iotas = sem("iotas")
        choosing = sem("choosing")
        group_exp = sem("group_exp")
        diff_exp = sem("diff_exp")
        counted = sem("counted")
        hot = sem("hot")
        table_step = sem("table_step")
        listed = sem("listed")

        with nc.Block(no_gpsimd_drain=True) as block:

            @block.sync
            def _(sp):
                sp.dma_start(W2[0], w2_v[0]).then_inc(expert_w[0][2], 16)
                sp.dma_start(W1[1], w1_v[1]).then_inc(expert_w[1][0], 16)
                sp.dma_start(W3[1], w3_v[1]).then_inc(expert_w[1][1], 16)
                sp.dma_start(W2[1], w2_v[1]).then_inc(expert_w[1][2], 16)

            @block.gpsimd
            def _(pool):
                small_ints = dict(allow_small_or_imprecise_dtypes=True)
                pool.iota(iota, [[1, COLS]], base=0, channel_multiplier=0, **small_ints).then_inc(iotas, 1)
                pool.iota(iota_p1, [[1, 1]], base=1, channel_multiplier=1, **small_ints).then_inc(iotas, 1)
                for k in range(2):
                    pool.iota(pair_code[k], [[2 * P, NT]], base=1 + k, channel_multiplier=2, **small_ints).then_inc(iotas, 1)
                pool.iota(past, [[P, NBLK - 1], [0, NE]], base=P, channel_multiplier=0, **small_ints).then_inc(iotas, 1)
                pool.memset(ones, 1.0).then_inc(iotas, 1)
                pool.wait_ge(iotas, 6)
                pool.affine_select(out=before, in_=ones, compare_op=ALU.is_gt, fill=0.0, base=0,
                                   pattern=[[1, P]], channel_multiplier=-1).then_inc(iotas, 1)

            @block.scalar
            def _(act):
                act.wait_ge(choosing, 2)
                act.activation(e4, d4, ACT.Exp).then_inc(group_exp, 1)
                act.wait_ge(choosing, 19)
                act.activation(e_diff, e_diff, ACT.Exp).then_inc(diff_exp, 1)

            @block.tensor
            def _(pe):
                pe.wait_ge(iotas, 7)
                pe.wait_ge(choosing, 28)
                for m in range(NT):
                    pe.matmul(ps[:, 0, m * NE:(m + 1) * NE], before, chosen[:, m], start=True, stop=(m == 0))
                    for j in range(m):
                        pe.matmul(ps[:, 0, m * NE:(m + 1) * NE], ones, chosen[:, j], start=False, stop=(j == m - 1))
                for j in range(NT):
                    mm = pe.matmul(ps[:, 1, 0:NE], ones, chosen[:, j], start=(j == 0), stop=(j == NT - 1))
                mm.then_inc(counted, 1)
                for n in range(PAIRS // P):
                    pe.wait_ge(hot, 2 * n + 2)
                    pe.matmul(ps[:, 2, 0:COLS], of_slot[n % NOH], of_column[n % NOH],
                              start=(n == 0), stop=(n == PAIRS // P - 1)).then_inc(table_step, 1)
                pe.wait_ge(listed, 1)
                pe.matmul(ps[0:1, 3, 0:P], over_col, ident, start=True, stop=True).then_inc(table_step, 1)

            @block.vector
            def _(dve):
                done = [0]

                def link(ins):
                    done[0] += 1
                    ins.then_inc(choosing, 1)
                    dve.wait_ge(choosing, done[0])

                wide = lambda a, n: a.unsqueeze(2).to_broadcast([P, NT, n])
                tall = lambda n: iota[:, 0:n].unsqueeze(1).to_broadcast([P, NT, n])

                def first_max(src, n, tmp, largest, index):
                    link(dve.tensor_tensor(tmp, src, wide(largest, n), ALU.is_equal))
                    link(dve.scalar_tensor_tensor(tmp, tmp, -float(COLS), tall(n), ALU.mult, ALU.add))
                    link(dve.tensor_reduce(index, tmp, AX.X, ALU.min))
                    link(dve.tensor_scalar(index, index, float(COLS), None, ALU.add))

                dve.wait_ge(iotas, 7)
                g = logits[:, :, 0:NG]
                link(dve.tensor_reduce(top[0], g, AX.X, ALU.max))
                link(dve.tensor_tensor(d4, g, wide(top[0], NG), ALU.subtract))
                first_max(g, NG, c4, top[0], which[0])
                link(dve.tensor_tensor(of_group, tall(NG), wide(which[0], NG), ALU.is_equal))
                link(dve.tensor_tensor(picked, logits[:, :, NG:].rearrange("p m (g e) -> p m g e", e=EPG),
                                       of_group.unsqueeze(3).to_broadcast([P, NT, NG, EPG]), ALU.mult))
                link(dve.tensor_reduce(sel[0], picked.rearrange("p m g e -> p m e g"), AX.X, ALU.add))
                link(dve.tensor_reduce(top[1], sel[0], AX.X, ALU.max))
                first_max(sel[0], EPG, c8, top[1], which[1])
                link(dve.tensor_tensor(of_choice, tall(EPG), wide(which[1], EPG), ALU.is_equal))
                link(dve.scalar_tensor_tensor(sel[1], of_choice, MASKED, sel[0], ALU.mult, ALU.add))
                link(dve.tensor_reduce(top[2], sel[1], AX.X, ALU.max))
                dve.wait_ge(group_exp, 1)
                link(dve.tensor_reduce(p_group, e4, AX.X, ALU.add))
                link(dve.tensor_tensor(e_diff, top[2], top[1], ALU.subtract))
                first_max(sel[1], EPG, c8, top[2], which[2])
                for k in range(2):
                    link(dve.scalar_tensor_tensor(expert[k], which[0], float(EPG), which[1 + k], ALU.mult, ALU.add))
                    link(dve.tensor_tensor(of_expert[k], tall(NE), wide(expert[k], NE), ALU.is_equal))
                link(dve.tensor_tensor(chosen, of_expert[0], of_expert[1], ALU.add))
                dve.wait_ge(diff_exp, 1)
                link(dve.scalar_tensor_tensor(gate[0], e_diff, 1.0, p_group, ALU.add, ALU.mult))
                link(dve.reciprocal(gate[0], gate[0]))
                link(dve.tensor_tensor(gate[1], gate[0], e_diff, ALU.mult))
                dve.wait_ge(counted, 1)
                for k in range(2):
                    link(dve.tensor_tensor(ranked, ps[:, 0, 0:NT * NE].rearrange("p (m e) -> p m e", e=NE), of_expert[k], ALU.mult))
                    link(dve.tensor_reduce(rank[k], ranked, AX.X, ALU.add))
                    link(dve.tensor_copy(rank_i, rank[k]))
                    link(dve.tensor_scalar(part_i, rank_i, 7, None, ALU.arith_shift_right))
                    link(dve.tensor_copy(column[k], part_i))
                    link(dve.scalar_tensor_tensor(column[k], column[k], float(NE), expert[k], ALU.mult, ALU.add))
                    link(dve.tensor_scalar(part_i, rank_i, P - 1, None, ALU.bitwise_and))
                    link(dve.tensor_copy(slot[k], part_i))
                for n in range(PAIRS // P):
                    k, m = n % 2, n // 2
                    if n >= NOH:
                        dve.wait_ge(table_step, n - NOH + 1)
                    dve.tensor_scalar(of_slot[n % NOH], iota[:, 0:P], slot[k][:, m:m + 1], None, ALU.is_equal).then_inc(hot, 1)
                    dve.tensor_scalar(of_column[n % NOH], iota, column[k][:, m:m + 1], pair_code[k][:, m:m + 1],
                                      ALU.is_equal, ALU.mult).then_inc(hot, 1)
                link(dve.tensor_tensor(over, ps[:, 1, 0:NE].unsqueeze(1).to_broadcast([P, NBLK - 1, NE]), past, ALU.is_gt))
                flags = over.rearrange("p b e -> p (b e)")
                link(dve.tensor_tensor_scan(over_at, flags, flags, 0.0, ALU.add, ALU.max))
                link(dve.scalar_tensor_tensor(over_sel, over_at, iota_p1, flags, ALU.is_equal, ALU.mult))
                link(dve.tensor_tensor(over_sel, over_sel, iota[:, NE:COLS], ALU.mult))
                dve.tensor_reduce(over_col, over_sel, AX.X, ALU.add).then_inc(listed, 1)
                link(dve.tensor_copy(over_n, over_at[0:1, (NBLK - 1) * NE - 1:(NBLK - 1) * NE]))
                dve.wait_ge(table_step, PAIRS // P)
                tab = ps[:, 2, 0:COLS]
                link(dve.tensor_scalar(unused, tab, 0.0, 4.0 * PAIRS, ALU.is_equal, ALU.mult))
                link(dve.scalar_tensor_tensor(pair_f, tab, -1.0, unused, ALU.add, ALU.add))
                link(dve.tensor_copy(slot_pair, pair_f))
                link(dve.tensor_scalar(slot_token, slot_pair, 1, None, ALU.arith_shift_right))
                dve.wait_ge(table_step, PAIRS // P + 1)
                link(dve.tensor_copy(over_list, ps[0:1, 3, 0:OVER + 1]))

        idx_token = [place(f"idx_token{i}", [P, 1], I32) for i in range(2)]
        idx_pair = [place(f"idx_pair{i}", [P, 1], I32) for i in range(2)]
        xg = [place(f"xg{i}", [P, D]) for i in range(2)]
        xT = [place(f"xT{i}", [P, KT, P]) for i in range(2)]
        act_out = [place(f"act_out{i}", [P, F]) for i in range(2)]
        hid = [place(f"hid{i}", [P, F]) for i in range(2)]
        hidT = [place(f"hidT{i}", [P, FT, P]) for i in range(2)]
        y = [place(f"y{i}", [P, D]) for i in range(2)]

        def expert_sems(tag):
            return {n: sem(f"{tag}_{n}") for n in
                    ("indexed", "turned", "xT_made", "gated", "upped", "silu", "hidden", "hid_turned", "hidT_made",
                     "downed", "y_made")} | {
                "gathered": [sem(f"{tag}_gathered{i}") for i in range(2)],
                "scattered": [sem(f"{tag}_scattered{i}") for i in range(2)]}

        def pe_turn_x(pe, s, n, b, rounds):
            pe.wait_ge(s["gathered"][b], 16 * rounds)
            pe.wait_ge(s["xT_made"], n)
            for k in range(KT):
                mm = pe.transpose(psf[:, k * P:(k + 1) * P], xg[b][:, k:D:KT], ident)
            mm.then_inc(s["turned"], 1)

        def pe_gate(pe, s, n, b):
            pe.wait_ge(s["xT_made"], n + 1)
            pe.wait_ge(s["silu"], n)
            for k in range(KT):
                mm = pe.matmul(ps[:, 2], xT[b][:, k], W1[b][:, k], start=(k == 0), stop=(k == KT - 1))
            mm.then_inc(s["gated"], 1)

        def pe_up(pe, s, n, b):
            pe.wait_ge(s["hidden"], n)
            for k in range(KT):
                mm = pe.matmul(ps[:, 3], xT[b][:, k], W3[b][:, k], start=(k == 0), stop=(k == KT - 1))
            mm.then_inc(s["upped"], 1)

        def pe_turn_hid(pe, s, n, b):
            pe.wait_ge(s["hidden"], n + 1)
            pe.wait_ge(s["hidT_made"], n)
            for k in range(FT):
                mm = pe.transpose(ps[:, 4, k * P:(k + 1) * P], hid[b][:, k:F:FT], ident)
            mm.then_inc(s["hid_turned"], 1)

        def pe_down(pe, s, n, b):
            pe.wait_ge(s["hidT_made"], n + 1)
            pe.wait_ge(s["y_made"], n)
            for h in range(2):
                for k in range(FT):
                    mm = pe.matmul(ps[:, 5 + h], hidT[b][:, k], W2[b][:, k, h * BANK:(h + 1) * BANK],
                                   start=(k == 0), stop=(k == FT - 1))
            mm.then_inc(s["downed"], 1)

        def act_xT(act, s, n, b):
            act.wait_ge(s["turned"], n + 1)
            act.wait_ge(s["upped"], n)
            act.activation(xT[b].rearrange("p k t -> p (k t)"), psf[:, 0:D], ACT.Copy).then_inc(s["xT_made"], 1)

        def act_silu(act, s, n, b):
            act.wait_ge(s["gated"], n + 1)
            act.wait_ge(s["hidden"], n)
            act.activation(act_out[b], ps[:, 2], ACT.Silu).then_inc(s["silu"], 1)

        def act_y(act, s, n, b, rounds):
            act.wait_ge(s["downed"], n + 1)
            act.wait_ge(s["scattered"][b], 16 * rounds)
            act.activation(y[b], psf[:, 5 * BANK:7 * BANK], ACT.Copy).then_inc(s["y_made"], 1)

        def dve_hid(dve, s, n, b):
            dve.wait_ge(s["upped"], n + 1)
            dve.wait_ge(s["silu"], n + 1)
            dve.wait_ge(s["hid_turned"], n)
            dve.tensor_tensor(hid[b], ps[:, 3], act_out[b], ALU.mult).then_inc(s["hidden"], 1)

        def dve_hidT(dve, s, n, b):
            dve.wait_ge(s["hid_turned"], n + 1)
            dve.wait_ge(s["downed"], n)
            dve.tensor_copy(hidT[b].rearrange("p k t -> p (k t)"), ps[:, 4]).then_inc(s["hidT_made"], 1)

        def pool_gather(pool, s, n, b, turned, rounds, col):
            if not (isinstance(rounds, int) and rounds == 0):
                pool.wait_ge(s["gathered"][b], 16 * rounds)
                pool.wait_ge(s["turned"], turned)
            pool.tensor_copy(idx_token[b], slot_token[:, bass.ds(col, 1)]).then_inc(s["indexed"], 1)

        def pool_gather_start(pool, s, b, indexed):
            pool.wait_ge(s["indexed"], indexed)
            start_step(pool)
            pool.indirect_dma_start(out=xg[b], out_offset=None, in_=xn2_rows,
                                    in_offset=bass.IndirectOffsetOnAxis(ap=idx_token[b].bitcast(U32), axis=0),
                                    bounds_check=S - 1, oob_is_err=False).then_inc(s["gathered"][b], 16)

        def pool_scatter(pool, s, n, b, rounds, col, indexed):
            if not (isinstance(rounds, int) and rounds == 0):
                pool.wait_ge(s["scattered"][b], 16 * rounds)
            pool.tensor_copy(idx_pair[b], slot_pair[:, bass.ds(col, 1)]).then_inc(s["indexed"], 1)
            pool.wait_ge(s["indexed"], indexed)
            pool.wait_ge(s["y_made"], n + 1)
            start_step(pool)
            pool.indirect_dma_start(out=y_rows, out_offset=bass.IndirectOffsetOnAxis(ap=idx_pair[b].bitcast(U32), axis=0),
                                    in_=y[b], in_offset=None,
                                    bounds_check=PAIRS - 1, oob_is_err=False).then_inc(s["scattered"][b], 16)

        s_e = expert_sems("first")
        cleared = sem("cleared")
        with nc.Block(no_gpsimd_drain=True) as block:

            @block.sync
            def _(sp):
                def load(w, wv, e, b, used, landed, n):
                    sp.wait_ge(s_e[used], n)
                    sp.dma_start(w[b], wv[bass.ds(e, 1)].rearrange("e p k f -> p (e k) f")).then_inc(expert_w[b][landed], 16)

                load(W1, w1_v, 2, 0, "gated", 0, 1)
                load(W3, w3_v, 2, 0, "upped", 1, 1)
                with sp.Fori(1, NE // 2 - 1) as i:
                    load(W1, w1_v, 2 * i + 1, 1, "gated", 0, 2 * i)
                    load(W3, w3_v, 2 * i + 1, 1, "upped", 1, 2 * i)
                    load(W2, w2_v, 2 * i, 0, "downed", 2, 2 * i - 1)
                    load(W1, w1_v, 2 * i + 2, 0, "gated", 0, 2 * i + 1)
                    load(W3, w3_v, 2 * i + 2, 0, "upped", 1, 2 * i + 1)
                    load(W2, w2_v, 2 * i + 1, 1, "downed", 2, 2 * i)
                load(W1, w1_v, NE - 1, 1, "gated", 0, NE - 2)
                load(W3, w3_v, NE - 1, 1, "upped", 1, NE - 2)
                load(W2, w2_v, NE - 2, 0, "downed", 2, NE - 3)
                load(W2, w2_v, NE - 1, 1, "downed", 2, NE - 2)

            @block.gpsimd
            def _(pool):
                pool.memset(xg[0], 0.0).then_inc(cleared, 1)
                pool.memset(xg[1], 0.0).then_inc(cleared, 1)
                pool.wait_ge(cleared, 2)
                for e in range(2):
                    pool_gather(pool, s_e, e, e, 0, 0, e)
                    pool_gather_start(pool, s_e, e, e + 1)
                pool_gather(pool, s_e, 2, 0, 1, 1, 2)
                pool_gather_start(pool, s_e, 0, 3)
                pool_scatter(pool, s_e, 0, 0, 0, 0, 4)
                pool_gather(pool, s_e, 3, 1, 2, 1, 3)
                pool_gather_start(pool, s_e, 1, 5)
                pool_scatter(pool, s_e, 1, 1, 0, 1, 6)
                with pool.Fori(1, NE // 2 - 1) as i:
                    for b in range(2):
                        n = 2 * i + b
                        pool_gather(pool, s_e, n + 2, b, n + 1, i + 1, n + 2)
                        pool_gather_start(pool, s_e, b, 2 * n + 3)
                        pool_scatter(pool, s_e, n, b, i, n, 2 * n + 4)
                for b in range(2):
                    n = NE - 2 + b
                    pool_scatter(pool, s_e, n, b, NE // 2 - 1, n, 2 * NE - 1 + b)
                for b in range(2):
                    pool.wait_ge(s_e["scattered"][b], 16 * (NE // 2))

            @block.tensor
            def _(pe):
                def expert_steps(e, b, rounds, pair):
                    pe.wait_ge(expert_w[b][0], 16 * rounds)
                    pe_gate(pe, s_e, e, b)
                    if pair != "first":
                        pe_turn_hid(pe, s_e, e - 1, 1 - b)
                    pe.wait_ge(expert_w[b][1], 16 * rounds)
                    pe_up(pe, s_e, e, b)
                    if pair != "last":
                        pe_turn_x(pe, s_e, e + 1, 1 - b, rounds + b)
                    if pair != "first":
                        pe.wait_ge(expert_w[1 - b][2], 16 * (rounds - 1 + b))
                        pe_down(pe, s_e, e - 1, 1 - b)

                pe_turn_x(pe, s_e, 0, 0, 1)
                expert_steps(0, 0, 1, "first")
                with pe.Fori(0, NE // 2 - 1) as i:
                    expert_steps(2 * i + 1, 1, i + 1, "")
                    expert_steps(2 * i + 2, 0, i + 2, "")
                expert_steps(NE - 1, 1, NE // 2, "last")
                pe_turn_hid(pe, s_e, NE - 1, 1)
                pe.wait_ge(expert_w[1][2], 16 * (NE // 2))
                pe_down(pe, s_e, NE - 1, 1)

            @block.scalar
            def _(act):
                act_xT(act, s_e, 0, 0)
                act_silu(act, s_e, 0, 0)
                act_xT(act, s_e, 1, 1)
                with act.Fori(0, NE // 2 - 1) as i:
                    act_silu(act, s_e, 2 * i + 1, 1)
                    act_xT(act, s_e, 2 * i + 2, 0)
                    act_y(act, s_e, 2 * i, 0, i)
                    act_silu(act, s_e, 2 * i + 2, 0)
                    act_xT(act, s_e, 2 * i + 3, 1)
                    act_y(act, s_e, 2 * i + 1, 1, i)
                act_silu(act, s_e, NE - 1, 1)
                act_y(act, s_e, NE - 2, 0, NE // 2 - 1)
                act_y(act, s_e, NE - 1, 1, NE // 2 - 1)

            @block.vector
            def _(dve):
                dve_hid(dve, s_e, 0, 0)
                with dve.Fori(0, NE // 2 - 1) as i:
                    dve_hidT(dve, s_e, 2 * i, 0)
                    dve_hid(dve, s_e, 2 * i + 1, 1)
                    dve_hidT(dve, s_e, 2 * i + 1, 1)
                    dve_hid(dve, s_e, 2 * i + 2, 0)
                dve_hidT(dve, s_e, NE - 2, 0)
                dve_hid(dve, s_e, NE - 1, 1)
                dve_hidT(dve, s_e, NE - 1, 1)

        s_o = expert_sems("over")
        over_w = [sem(f"over_w{i}") for i in range(3)]
        with nc.Block(no_gpsimd_drain=True) as block:

            def each_block(eng, body):
                n_over = eng.value_load(over_n[0:1, 0:1], min_val=0, max_val=OVER)
                with eng.Fori(0, OVER) as n:
                    with eng.If(n < n_over):
                        body(n)

            def column_of(eng, n):
                return eng.value_load(over_list[0:1, bass.ds(n, 1)], min_val=0, max_val=COLS - 1)

            @block.sync
            def _(sp):
                def body(n):
                    e = column_of(sp, n) % NE
                    for j, (w, wv, used) in enumerate(((W1, w1_v, "gated"), (W3, w3_v, "upped"), (W2, w2_v, "downed"))):
                        sp.wait_ge(s_o[used], n)
                        sp.dma_start(w[0], wv[bass.ds(e, 1)].rearrange("e p k f -> p (e k) f")).then_inc(over_w[j], 16)
                each_block(sp, body)

            @block.gpsimd
            def _(pool):
                def body(n):
                    col = column_of(pool, n)
                    pool_gather(pool, s_o, n, 0, n, n, col)
                    pool_gather_start(pool, s_o, 0, 2 * n + 1)
                    pool_scatter(pool, s_o, n, 0, n, col, 2 * n + 2)
                    pool.wait_ge(s_o["scattered"][0], 16 * n + 16)
                each_block(pool, body)

            @block.tensor
            def _(pe):
                def body(n):
                    pe_turn_x(pe, s_o, n, 0, n + 1)
                    pe.wait_ge(over_w[0], 16 * n + 16)
                    pe_gate(pe, s_o, n, 0)
                    pe.wait_ge(over_w[1], 16 * n + 16)
                    pe_up(pe, s_o, n, 0)
                    pe_turn_hid(pe, s_o, n, 0)
                    pe.wait_ge(over_w[2], 16 * n + 16)
                    pe_down(pe, s_o, n, 0)
                each_block(pe, body)

            @block.scalar
            def _(act):
                def body(n):
                    act_xT(act, s_o, n, 0)
                    act_silu(act, s_o, n, 0)
                    act_y(act, s_o, n, 0, n)
                each_block(act, body)

            @block.vector
            def _(dve):
                def body(n):
                    dve_hid(dve, s_o, n, 0)
                    dve_hidT(dve, s_o, n, 0)
                each_block(dve, body)

        y_tiles = y_rows.rearrange("(m p k) d -> m p (k d)", p=P, k=2)
        yy = [at(f"yy{m}", 8 * m, [P, 2, D]) for m in range(NT)]
        y_back = [sem(f"y_back{m}") for m in range(NT)]
        combined = sem("combined")
        out_stored = sem("out_stored")
        with nc.Block(no_gpsimd_drain=True) as block:

            @block.sync
            def _(sp):
                for m in range(NT):
                    sp.dma_start(yy[m].rearrange("p k d -> p (k d)"), y_tiles[m]).then_inc(y_back[m], 16)

            @block.vector
            def _(dve):
                for m in range(NT):
                    dve.wait_ge(y_back[m], 16)
                    for k in range(2):
                        if k:
                            dve.wait_ge(combined, 2 * m + 1)
                        dve.scalar_tensor_tensor(x2[:, m], yy[m][:, k], gate[k][:, m:m + 1], x2[:, m],
                                                 ALU.mult, ALU.add).then_inc(combined, 1)

            @block.scalar
            def _(act):
                for m in range(NT):
                    act.wait_ge(combined, 2 * m + 2)
                    act.dma_start(outv[m], x2[:, m]).then_inc(out_stored, 16)
                act.wait_ge(out_stored, 16 * NT)

        return dict(locals())


_INS = ['x', 'norm_mix_w', 'w_in', 'conv_w', 'q_norm_w', 'k_norm_w', 'group_norm_conv_w', 'group_norm_attn_w',
        'w_out', 'norm_ffn_w', 'w_group', 'b_group', 'w_expert', 'b_expert', 'w1', 'w3', 'w2']
_OUTS = [((1, 1024, 1024), 'float32')]


def build(nc, shapes):
    args = []
    for name in _INS:
        args.append(nc.dram_tensor(f"in_{name}_dram", shapes[name], F32, kind="ExternalInput").ap())
    for i, (shape, dtype) in enumerate(_OUTS):
        args.append(nc.dram_tensor(f"out_{i}_dram", shape, F32, kind="ExternalOutput").ap())
    return hymba_moe_layer(nc, *args)


def kernel(**inputs):
    import numpy as _np
    import concourse.bacc as _bacc
    from concourse.bass_utils import run_bass_kernel_spmd as _run

    nc = _bacc.Bacc("TRN2", target_bir_lowering=False, num_devices=1)
    arrays = {f"in_{name}_dram": _np.ascontiguousarray(inputs[name]) for name in _INS}
    build(nc, {name: inputs[name].shape for name in _INS})
    r = _run(nc, [arrays], core_ids=[0])
    return r.results[0]["out_0_dram"]
```
